# Optimizing a Trainium2 kernel written in Bass

```python
import math
import jax, jax.numpy as jnp
from jax import lax
import numpy as np

D_MODEL = 1024
BATCH = 1
SEQ = 256
DEPTH = 1

HEAD_DIM = 64
D_MIX = D_MODEL
MOBA_HEADS = (D_MIX // 2) // HEAD_DIM
NSA_HEADS = (D_MIX // 2) // HEAD_DIM
NSA_KV_GROUPS = 2
MOBA_BLOCK = 256
MOBA_TOPK = 3
MOBA_QCHUNK = 32
NSA_CMP_LEN = 32
NSA_CMP_STRIDE = 16
NSA_CMP_HIDDEN = 256
NSA_SLC_BLOCK = 64
NSA_SLC_TOPN = 16
NSA_WINDOW = 512
NSA_QCHUNK = 64
NSA_N_GATES = 3
REL_BUCKETS = 32
REL_MAX_EXACT = REL_BUCKETS // 2
REL_MAX_DIST = 128
N_BIAS_HEADS = MOBA_HEADS + NSA_HEADS
D_FF = 2816
RMS_EPS = 1e-6
PROJ_SIZES = (MOBA_HEADS * HEAD_DIM,) * 3 + (NSA_HEADS * HEAD_DIM,) + (NSA_KV_GROUPS * HEAD_DIM,) * 6 + (NSA_HEADS * NSA_N_GATES,)
D_IN_PROJ = sum(PROJ_SIZES)
PROJ_SPLITS = tuple(int(s) for s in np.cumsum(PROJ_SIZES)[:-1])


def rmsnorm(x, g):
    xf = x.astype(jnp.float32)
    y = xf * lax.rsqrt(jnp.mean(xf * xf, axis=-1, keepdims=True) + RMS_EPS)
    return (y * g.astype(jnp.float32)).astype(x.dtype)

def swiglu(h, w_gate, w_up, w_down):
    return (jax.nn.silu(h @ w_gate) * (h @ w_up)) @ w_down

def rel_bucket(dist):
    n = jnp.maximum(dist, 0)
    is_small = n < REL_MAX_EXACT
    nf = jnp.maximum(n, 1).astype(jnp.float32)
    large = REL_MAX_EXACT + (jnp.log(nf / REL_MAX_EXACT) / math.log(REL_MAX_DIST / REL_MAX_EXACT) * (REL_BUCKETS - REL_MAX_EXACT)).astype(jnp.int32)
    return jnp.where(is_small, n, jnp.minimum(large, REL_BUCKETS - 1))

def masked_softmax(logits, mask):
    lf = jnp.where(mask, logits.astype(jnp.float32), -jnp.inf)
    m = jnp.max(lf, axis=-1, keepdims=True)
    m = jnp.where(jnp.isfinite(m), m, 0.0)
    p = jnp.exp(lf - m)
    den = jnp.sum(p, axis=-1, keepdims=True)
    return p / jnp.where(den > 0, den, 1.0)

def slc_overlap(n_cmp, n_slc):
    r = NSA_SLC_BLOCK // NSA_CMP_STRIDE
    mc = NSA_CMP_LEN // NSA_CMP_STRIDE
    j = np.arange(n_slc)
    offs = (np.arange(r)[:, None] + np.arange(mc)[None, :]).reshape(-1)
    c = r * j[:, None] + offs[None, :]
    w = np.zeros((n_slc * r + mc, n_slc), np.float32)
    np.add.at(w, (c, np.broadcast_to(j[:, None], c.shape)), 1.0)
    return w[:n_cmp]

def moba_attention(q, k, v, tab):
    B, H, S, dh = q.shape
    nblk = -(-S // MOBA_BLOCK)
    s_pad = nblk * MOBA_BLOCK
    pad = ((0, 0), (0, 0), (0, s_pad - S), (0, 0))
    kp = jnp.pad(k, pad)
    vp = jnp.pad(v, pad)
    k_blocks = kp.reshape(B, H, nblk, MOBA_BLOCK, dh)
    v_blocks = vp.reshape(B, H, nblk, MOBA_BLOCK, dh)
    k_mean = jnp.mean(k_blocks.astype(jnp.float32), axis=3).astype(k.dtype)
    topk = min(MOBA_TOPK, nblk)
    n_sel = topk * MOBA_BLOCK
    C = MOBA_QCHUNK
    n_chunks = S // C
    q_chunks = q.reshape(B, H, n_chunks, C, dh).transpose(2, 0, 1, 3, 4)
    bi = jnp.arange(B)[:, None, None, None]
    hi = jnp.arange(H)[None, :, None, None]
    blk_ids = jnp.arange(nblk)
    offs = jnp.arange(MOBA_BLOCK)
    scale = dh ** -0.5

    def chunk_fn(args):
        qc, c = args
        t = c * C + jnp.arange(C)
        cur = (c * C) // MOBA_BLOCK
        gate = jnp.einsum('bhcd,bhnd->bhcn', qc, k_mean).astype(jnp.float32)
        gate = jnp.where(blk_ids < cur, gate, -jnp.inf)
        _, sel = lax.top_k(gate, topk)
        k_sel = k_blocks[bi, hi, sel].reshape(B, H, C, n_sel, dh)
        v_sel = v_blocks[bi, hi, sel].reshape(B, H, C, n_sel, dh)
        pos_sel = (sel[..., None] * MOBA_BLOCK + offs).reshape(B, H, C, n_sel)
        mask_sel = jnp.repeat(sel < cur, MOBA_BLOCK, axis=-1)
        bias_sel = tab[hi, rel_bucket(t[:, None] - pos_sel)]
        k_own = lax.dynamic_slice_in_dim(kp, cur * MOBA_BLOCK, MOBA_BLOCK, axis=2)
        v_own = lax.dynamic_slice_in_dim(vp, cur * MOBA_BLOCK, MOBA_BLOCK, axis=2)
        d_own = t[:, None] - (cur * MOBA_BLOCK + offs)[None, :]
        mask_own = jnp.broadcast_to(d_own >= 0, (B, H, C, MOBA_BLOCK))
        bias_own = tab[:, rel_bucket(d_own)]
        lg_sel = jnp.einsum('bhcd,bhckd->bhck', qc, k_sel).astype(jnp.float32) * scale + bias_sel
        lg_own = jnp.einsum('bhcd,bhkd->bhck', qc, k_own).astype(jnp.float32) * scale + bias_own
        p = masked_softmax(jnp.concatenate([lg_sel, lg_own], axis=-1), jnp.concatenate([mask_sel, mask_own], axis=-1)).astype(v.dtype)
        return jnp.einsum('bhck,bhckd->bhcd', p[..., :n_sel], v_sel) + jnp.einsum('bhck,bhkd->bhcd', p[..., n_sel:], v_own)

    out = lax.map(chunk_fn, (q_chunks, jnp.arange(n_chunks)))
    return out.transpose(1, 2, 0, 3, 4).reshape(B, H, S, dh)

def nsa_attention(q, kc_raw, vc_raw, ks, vs, kw, vw, gates, tab, pos_k, w1_k, w2_k, pos_v, w1_v, w2_v):
    B, H, S, dh = q.shape
    G = kc_raw.shape[1]
    R = H // G
    scale = dh ** -0.5
    n_cmp = (S - NSA_CMP_LEN) // NSA_CMP_STRIDE + 1
    idx = (np.arange(n_cmp)[:, None] * NSA_CMP_STRIDE + np.arange(NSA_CMP_LEN)[None, :]).astype(np.int32)

    def compress(raw, pos, w1, w2):
        blocks = raw[:, :, idx] + pos
        return jax.nn.silu(blocks.reshape(B, G, n_cmp, NSA_CMP_LEN * dh) @ w1) @ w2

    k_cmp = compress(kc_raw, pos_k, w1_k, w2_k)
    v_cmp = compress(vc_raw, pos_v, w1_v, w2_v)
    cmp_end = jnp.asarray(np.arange(n_cmp, dtype=np.int32) * NSA_CMP_STRIDE + NSA_CMP_LEN - 1)
    n_slc = S // NSA_SLC_BLOCK
    n_top = min(NSA_SLC_TOPN, n_slc)
    n_sel = n_top * NSA_SLC_BLOCK
    overlap = jnp.asarray(slc_overlap(n_cmp, n_slc))
    ks_blocks = ks.reshape(B, G, n_slc, NSA_SLC_BLOCK, dh)
    vs_blocks = vs.reshape(B, G, n_slc, NSA_SLC_BLOCK, dh)
    wpad = ((0, 0), (0, 0), (NSA_WINDOW, 0), (0, 0))
    kw_pad = jnp.pad(kw, wpad)
    vw_pad = jnp.pad(vw, wpad)
    tab_g = tab.reshape(G, R, REL_BUCKETS)
    C = NSA_QCHUNK
    n_chunks = S // C
    q_chunks = q.reshape(B, G, R, n_chunks, C, dh).transpose(3, 0, 1, 2, 4, 5)
    g_chunks = gates.reshape(B, G, R, n_chunks, C, NSA_N_GATES).transpose(3, 0, 1, 2, 4, 5)
    bi = jnp.arange(B)[:, None, None, None]
    gi = jnp.arange(G)[None, :, None, None]
    gi5 = jnp.arange(G)[:, None, None, None]
    ri5 = jnp.arange(R)[:, None, None]
    slc_ids = jnp.arange(n_slc)
    offs = jnp.arange(NSA_SLC_BLOCK)
    win_offs = jnp.arange(NSA_WINDOW + C)

    def chunk_fn(args):
        qc, gc, c = args
        t = c * C + jnp.arange(C)
        d_cmp = t[:, None] - cmp_end[None, :]
        lg = jnp.einsum('bgrcd,bgnd->bgrcn', qc, k_cmp).astype(jnp.float32) * scale + tab_g[:, :, rel_bucket(d_cmp)]
        p_cmp = masked_softmax(lg, d_cmp >= 0)
        o_cmp = jnp.einsum('bgrcn,bgnd->bgrcd', p_cmp.astype(v_cmp.dtype), v_cmp)
        imp = jnp.einsum('bgrcn,nj->bgcj', p_cmp, overlap)
        cur = t // NSA_SLC_BLOCK
        forced = (slc_ids[None, :] == 0) | (slc_ids[None, :] == cur[:, None]) | (slc_ids[None, :] == cur[:, None] - 1)
        allowed = slc_ids[None, :] <= cur[:, None]
        score = jnp.where(forced, jnp.inf, jnp.where(allowed, imp, -jnp.inf))
        _, sel = lax.top_k(score, n_top)
        k_sel = ks_blocks[bi, gi, sel].reshape(B, G, C, n_sel, dh)
        v_sel = vs_blocks[bi, gi, sel].reshape(B, G, C, n_sel, dh)
        pos_sel = (sel[..., None] * NSA_SLC_BLOCK + offs).reshape(B, G, C, n_sel)
        d_sel = t[:, None] - pos_sel
        lg = jnp.einsum('bgrcd,bgckd->bgrck', qc, k_sel).astype(jnp.float32) * scale + tab_g[gi5, ri5, rel_bucket(d_sel)[:, :, None]]
        p_slc = masked_softmax(lg, (d_sel >= 0)[:, :, None]).astype(v_sel.dtype)
        o_slc = jnp.einsum('bgrck,bgckd->bgrcd', p_slc, v_sel)
        k_win = lax.dynamic_slice_in_dim(kw_pad, c * C, NSA_WINDOW + C, axis=2)
        v_win = lax.dynamic_slice_in_dim(vw_pad, c * C, NSA_WINDOW + C, axis=2)
        pos_win = c * C - NSA_WINDOW + win_offs
        d_win = t[:, None] - pos_win[None, :]
        mask_win = (pos_win[None, :] >= 0) & (d_win >= 0) & (d_win < NSA_WINDOW)
        lg = jnp.einsum('bgrcd,bgkd->bgrck', qc, k_win).astype(jnp.float32) * scale + tab_g[:, :, rel_bucket(d_win)]
        p_win = masked_softmax(lg, mask_win).astype(v_win.dtype)
        o_win = jnp.einsum('bgrck,bgkd->bgrcd', p_win, v_win)
        return gc[..., 0:1] * o_cmp + gc[..., 1:2] * o_slc + gc[..., 2:3] * o_win

    out = lax.map(chunk_fn, (q_chunks, g_chunks, jnp.arange(n_chunks)))
    return out.transpose(1, 2, 3, 0, 4, 5).reshape(B, H, S, dh)

def hybrid_mixer(h, w_in, pos_k, w1_k, w2_k, pos_v, w1_v, w2_v, w_out, rel_bias):
    B, S, _ = h.shape
    proj = h @ w_in
    qa, ka, va, qb, kcb, vcb, ksb, vsb, kwb, vwb, gb = jnp.split(proj, PROJ_SPLITS, axis=-1)

    def heads(t, n):
        return t.reshape(B, S, n, HEAD_DIM).transpose(0, 2, 1, 3)

    out_a = moba_attention(heads(qa, MOBA_HEADS), heads(ka, MOBA_HEADS), heads(va, MOBA_HEADS), rel_bias[:, :MOBA_HEADS].T)
    gates = jax.nn.sigmoid(gb.astype(jnp.float32)).astype(h.dtype).reshape(B, S, NSA_HEADS, NSA_N_GATES).transpose(0, 2, 1, 3)
    out_b = nsa_attention(heads(qb, NSA_HEADS), heads(kcb, NSA_KV_GROUPS), heads(vcb, NSA_KV_GROUPS), heads(ksb, NSA_KV_GROUPS), heads(vsb, NSA_KV_GROUPS), heads(kwb, NSA_KV_GROUPS), heads(vwb, NSA_KV_GROUPS), gates, rel_bias[:, MOBA_HEADS:].T, pos_k, w1_k, w2_k, pos_v, w1_v, w2_v)
    o = jnp.concatenate([out_a.transpose(0, 2, 1, 3).reshape(B, S, MOBA_HEADS * HEAD_DIM), out_b.transpose(0, 2, 1, 3).reshape(B, S, NSA_HEADS * HEAD_DIM)], axis=-1)
    return o @ w_out

def first_inputs(seed: int = 0) -> dict:
    key = jax.random.key(seed)
    ks = jax.random.split(key, 20)

    def nrm(k, shape, s):
        return jax.random.normal(k, shape, jnp.float32) * s

    def gain(k, shape):
        return 1.0 + 0.05 * jax.random.normal(k, shape, jnp.float32)

    L = DEPTH
    flat_cmp = NSA_CMP_LEN * HEAD_DIM
    return {
        'x': nrm(ks[0], (BATCH, SEQ, D_MODEL), 1.0),
        'norm_ffn1': gain(ks[1], (L, D_MODEL)),
        'w_ffn1_gate': nrm(ks[2], (L, D_MODEL, D_FF), D_MODEL ** -0.5),
        'w_ffn1_up': nrm(ks[3], (L, D_MODEL, D_FF), D_MODEL ** -0.5),
        'w_ffn1_down': nrm(ks[4], (L, D_FF, D_MODEL), D_FF ** -0.5),
        'norm_mix': gain(ks[5], (L, D_MODEL)),
        'w_in': nrm(ks[6], (L, D_MODEL, D_IN_PROJ), D_MODEL ** -0.5),
        'cmp_pos_k': nrm(ks[7], (L, NSA_CMP_LEN, HEAD_DIM), 0.5),
        'cmp_w1_k': nrm(ks[8], (L, flat_cmp, NSA_CMP_HIDDEN), flat_cmp ** -0.5),
        'cmp_w2_k': nrm(ks[9], (L, NSA_CMP_HIDDEN, HEAD_DIM), NSA_CMP_HIDDEN ** -0.5),
        'cmp_pos_v': nrm(ks[10], (L, NSA_CMP_LEN, HEAD_DIM), 0.5),
        'cmp_w1_v': nrm(ks[11], (L, flat_cmp, NSA_CMP_HIDDEN), flat_cmp ** -0.5),
        'cmp_w2_v': nrm(ks[12], (L, NSA_CMP_HIDDEN, HEAD_DIM), NSA_CMP_HIDDEN ** -0.5),
        'w_out': nrm(ks[13], (L, D_MIX, D_MODEL), D_MIX ** -0.5),
        'norm_ffn2': gain(ks[14], (L, D_MODEL)),
        'w_ffn2_gate': nrm(ks[15], (L, D_MODEL, D_FF), D_MODEL ** -0.5),
        'w_ffn2_up': nrm(ks[16], (L, D_MODEL, D_FF), D_MODEL ** -0.5),
        'w_ffn2_down': nrm(ks[17], (L, D_FF, D_MODEL), D_FF ** -0.5),
        'rel_bias': nrm(ks[18], (REL_BUCKETS, N_BIAS_HEADS), 0.5),
        'norm_final': gain(ks[19], (D_MODEL,)),
    }

def first_block(x, norm_ffn1, w_ffn1_gate, w_ffn1_up, w_ffn1_down, norm_mix, w_in, cmp_pos_k, cmp_w1_k, cmp_w2_k, cmp_pos_v, cmp_w1_v, cmp_w2_v, w_out, norm_ffn2, w_ffn2_gate, w_ffn2_up, w_ffn2_down, rel_bias, norm_final):
    for l in range(DEPTH):
        x = x + 0.5 * swiglu(rmsnorm(x, norm_ffn1[l]), w_ffn1_gate[l], w_ffn1_up[l], w_ffn1_down[l])
        x = x + hybrid_mixer(rmsnorm(x, norm_mix[l]), w_in[l], cmp_pos_k[l], cmp_w1_k[l], cmp_w2_k[l], cmp_pos_v[l], cmp_w1_v[l], cmp_w2_v[l], w_out[l], rel_bias)
        x = x + 0.5 * swiglu(rmsnorm(x, norm_ffn2[l]), w_ffn2_gate[l], w_ffn2_up[l], w_ffn2_down[l])
    return rmsnorm(x, norm_final)


DEPTH_2 = 2

CHUNK = 64
N_MEM = 256
MIX_WIDTH = (D_MODEL * 3) // 4
N_MIX_HEADS = MIX_WIDTH // HEAD_DIM
MEM_WIDTH = D_MODEL - MIX_WIDTH
N_MEM_HEADS = MEM_WIDTH // HEAD_DIM
DECAY_LORA = 64
AAA_LORA = 64
GATE_LORA = 128
Q_BLOCK = 128
N_MIXERS = 2
N_RWKV = (DEPTH_2 + 1) // 2
N_SB = DEPTH_2 // 2
ALPHA = (2 * DEPTH_2) ** 0.25
BETA = (8 * DEPTH_2) ** -0.25
LN_EPS = 1e-5
LNX_EPS = 64e-5
RWKV_SHIFT = 3 * MIX_WIDTH + DECAY_LORA + AAA_LORA + GATE_LORA
RWKV_IN = RWKV_SHIFT + MEM_WIDTH
SB_IN = 3 * MIX_WIDTH + MEM_WIDTH


def layer_norm(x, g, b):
    xf = x.astype(jnp.float32)
    mu = jnp.mean(xf, axis=-1, keepdims=True)
    var = jnp.mean(jnp.square(xf - mu), axis=-1, keepdims=True)
    return ((xf - mu) * lax.rsqrt(var + LN_EPS) * g + b).astype(x.dtype)

def swiglu_2(x, w_gate, w_up, w_down):
    return (jax.nn.silu(x @ w_gate) * (x @ w_up)) @ w_down

def split_heads(t):
    b, s, _ = t.shape
    return t.reshape(b, s, -1, HEAD_DIM).transpose(0, 2, 1, 3)

def merge_heads(t):
    b, h, s, d = t.shape
    return t.transpose(0, 2, 1, 3).reshape(b, s, h * d)

def token_shift(p, mu):
    prev = jnp.pad(p, ((0, 0), (1, 0), (0, 0)))[:, :-1]
    return p + (prev - p) * mu

def memory_attention(mq, mem_k, mem_v):
    q = split_heads(mq)
    scores = jnp.einsum('bhsd,bhmd->bhsm', q, mem_k).astype(jnp.float32) / math.sqrt(HEAD_DIM)
    p = jax.nn.softmax(scores, axis=-1).astype(mq.dtype)
    return merge_heads(jnp.einsum('bhsm,bhmd->bhsd', p, mem_v))

def rwkv7_mix(z_in, mu, w0, w_up, a0, a_up, g_up, k_k, k_a, r_k, lnx_g, lnx_b):
    bsz, seq, _ = z_in.shape
    dt = z_in.dtype
    z = token_shift(z_in, mu)
    c = MIX_WIDTH
    r = z[..., :c]
    k = z[..., c:2 * c]
    v = z[..., 2 * c:3 * c]
    o = 3 * c
    dw = z[..., o:o + DECAY_LORA]
    o += DECAY_LORA
    da = z[..., o:o + AAA_LORA]
    o += AAA_LORA
    dg = z[..., o:o + GATE_LORA]
    w = -jax.nn.softplus(-(w0 + jnp.tanh(dw) @ w_up)) - 0.5
    a = jax.nn.sigmoid(a0 + da @ a_up)
    g = jax.nn.sigmoid(dg) @ g_up

    def hs(t):
        return t.astype(jnp.float32).reshape(bsz, seq, N_MIX_HEADS, HEAD_DIM)

    kk = hs(k * k_k)
    kk = kk * lax.rsqrt(jnp.maximum(jnp.sum(kk * kk, axis=-1, keepdims=True), 1e-24))
    k = hs(k * (1.0 + (a - 1.0) * k_a))
    r, v, a = hs(r), hs(v), hs(a)
    decay = jnp.exp(-jnp.exp(hs(w)))

    n_chunks = seq // CHUNK

    def to_chunks(t):
        return t.transpose(1, 0, 2, 3).reshape(n_chunks, CHUNK, bsz, N_MIX_HEADS, HEAD_DIM)

    xs = (to_chunks(r), to_chunks(decay), to_chunks(k), to_chunks(v), to_chunks(kk), to_chunks(kk * a))

    def step(state, inp):
        r_t, w_t, k_t, v_t, kk_t, b_t = inp
        sa = jnp.einsum('bhij,bhj->bhi', state, kk_t)
        state = (state * w_t[:, :, None, :] - sa[..., :, None] * b_t[..., None, :]
                 + v_t[..., :, None] * k_t[..., None, :])
        return state, jnp.einsum('bhij,bhj->bhi', state, r_t)

    def chunk_step(state, chunk_inp):
        return lax.scan(step, state, chunk_inp)

    state0 = jnp.zeros((bsz, N_MIX_HEADS, HEAD_DIM, HEAD_DIM), jnp.float32)
    _, out = lax.scan(chunk_step, state0, xs)
    out = out.reshape(seq, bsz, N_MIX_HEADS, HEAD_DIM).transpose(1, 0, 2, 3)
    m = jnp.mean(out, axis=-1, keepdims=True)
    var = jnp.mean(jnp.square(out - m), axis=-1, keepdims=True)
    out = ((out - m) * lax.rsqrt(var + LNX_EPS)).reshape(bsz, seq, c) * lnx_g + lnx_b
    bonus = jnp.sum(r * k * r_k, axis=-1, keepdims=True) * v
    y = (out + bonus.reshape(bsz, seq, c)) * g
    return y.astype(dt)

def stick_breaking_mix(q, k, v):
    q, k, v = split_heads(q), split_heads(k), split_heads(v)
    seq = q.shape[2]
    scale = 1.0 / math.sqrt(HEAD_DIM)
    outs = []
    for blk in range(seq // Q_BLOCK):
        start = blk * Q_BLOCK
        end = start + Q_BLOCK
        kb = k[:, :, :end]
        vb = v[:, :, :end]
        z = jnp.einsum('bhtd,bhsd->bhts', q[:, :, start:end], kb).astype(jnp.float32) * scale
        t_pos = start + jnp.arange(Q_BLOCK)[:, None]
        s_pos = jnp.arange(end)[None, :]
        before = s_pos < t_pos
        log_keep = jnp.where(before, -jax.nn.softplus(z), 0.0)
        later = lax.cumsum(log_keep, axis=3, reverse=True) - log_keep
        att = jnp.where(before, jnp.exp(jax.nn.log_sigmoid(z) + later), 0.0)
        outs.append(jnp.einsum('bhts,bhsd->bhtd', att.astype(v.dtype), vb))
    return merge_heads(jnp.concatenate(outs, axis=2))

def second_inputs(seed: int = 0) -> dict:
    key = jax.random.key(seed)
    ks = jax.random.split(key, 32)
    f32 = jnp.float32
    d, f, c = D_MODEL, D_FF, MIX_WIDTH

    def nrm(k, shape, scale):
        return jax.random.normal(k, shape, f32) * scale

    return {
        "x": nrm(ks[0], (BATCH, SEQ, d), 1.0),
        "mem": nrm(ks[1], (BATCH, N_MEM, d), 1.0),
        "ffn1_w_gate": nrm(ks[2], (DEPTH_2, d, f), d ** -0.5),
        "ffn1_w_up": nrm(ks[3], (DEPTH_2, d, f), d ** -0.5),
        "ffn1_w_down": nrm(ks[4], (DEPTH_2, f, d), BETA * f ** -0.5),
        "ffn2_w_gate": nrm(ks[5], (DEPTH_2, d, f), d ** -0.5),
        "ffn2_w_up": nrm(ks[6], (DEPTH_2, d, f), d ** -0.5),
        "ffn2_w_down": nrm(ks[7], (DEPTH_2, f, d), BETA * f ** -0.5),
        "ln_g": 1.0 + nrm(ks[8], (DEPTH_2, 3, d), 0.02),
        "ln_b": nrm(ks[9], (DEPTH_2, 3, d), 0.02),
        "w_out": nrm(ks[10], (DEPTH_2, d, d), BETA * d ** -0.5),
        "w_mem_kv": nrm(ks[11], (d, 2 * MEM_WIDTH), d ** -0.5),
        "rwkv_w_in": nrm(ks[12], (N_RWKV, d, RWKV_IN), d ** -0.5),
        "rwkv_mu": jax.random.uniform(ks[13], (N_RWKV, RWKV_SHIFT), f32),
        "rwkv_w0": jax.random.uniform(ks[14], (N_RWKV, c), f32, -6.0, -1.0),
        "rwkv_w_up": nrm(ks[15], (N_RWKV, DECAY_LORA, c), 0.1 * DECAY_LORA ** -0.5),
        "rwkv_a0": nrm(ks[16], (N_RWKV, c), 0.5),
        "rwkv_a_up": nrm(ks[17], (N_RWKV, AAA_LORA, c), 0.5 * AAA_LORA ** -0.5),
        "rwkv_g_up": nrm(ks[18], (N_RWKV, GATE_LORA, c), GATE_LORA ** -0.5),
        "rwkv_k_k": 1.0 + nrm(ks[19], (N_RWKV, c), 0.1),
        "rwkv_k_a": 1.0 + nrm(ks[20], (N_RWKV, c), 0.1),
        "rwkv_r_k": nrm(ks[21], (N_RWKV, N_MIX_HEADS, HEAD_DIM), 0.1),
        "rwkv_lnx_g": 1.0 + nrm(ks[22], (N_RWKV, c), 0.02),
        "rwkv_lnx_b": nrm(ks[23], (N_RWKV, c), 0.02),
        "sb_w_in": nrm(ks[24], (N_SB, d, SB_IN), d ** -0.5),
    }

def second_block(x, mem, ffn1_w_gate, ffn1_w_up, ffn1_w_down, ffn2_w_gate, ffn2_w_up, ffn2_w_down,
              ln_g, ln_b, w_out, w_mem_kv, rwkv_w_in, rwkv_mu, rwkv_w0, rwkv_w_up, rwkv_a0,
              rwkv_a_up, rwkv_g_up, rwkv_k_k, rwkv_k_a, rwkv_r_k, rwkv_lnx_g, rwkv_lnx_b, sb_w_in):
    mem_kv = mem @ w_mem_kv
    mem_k = split_heads(mem_kv[..., :MEM_WIDTH])
    mem_v = split_heads(mem_kv[..., MEM_WIDTH:])
    c = MIX_WIDTH
    for i in range(DEPTH_2):
        x = layer_norm(ALPHA * x + 0.5 * swiglu_2(x, ffn1_w_gate[i], ffn1_w_up[i], ffn1_w_down[i]),
                       ln_g[i, 0], ln_b[i, 0])
        j = i // N_MIXERS
        if i % N_MIXERS == 0:
            proj = x @ rwkv_w_in[j]
            mix = rwkv7_mix(proj[..., :RWKV_SHIFT], rwkv_mu[j], rwkv_w0[j], rwkv_w_up[j],
                            rwkv_a0[j], rwkv_a_up[j], rwkv_g_up[j], rwkv_k_k[j], rwkv_k_a[j],
                            rwkv_r_k[j], rwkv_lnx_g[j], rwkv_lnx_b[j])
            mq = proj[..., RWKV_SHIFT:]
        else:
            proj = x @ sb_w_in[j]
            mix = stick_breaking_mix(proj[..., :c], proj[..., c:2 * c], proj[..., 2 * c:3 * c])
            mq = proj[..., 3 * c:]
        heads = jnp.concatenate([mix, memory_attention(mq, mem_k, mem_v)], axis=-1)
        x = layer_norm(ALPHA * x + heads @ w_out[i], ln_g[i, 1], ln_b[i, 1])
        x = layer_norm(ALPHA * x + 0.5 * swiglu_2(x, ffn2_w_gate[i], ffn2_w_up[i], ffn2_w_down[i]),
                       ln_g[i, 2], ln_b[i, 2])
    return x


def setup_inputs(seed=0):
    out = dict(first_inputs(seed))
    for name, value in second_inputs(seed + 1).items():
        if name != "x":
            out[name + "_2"] = value
    return out


def reference(
    x, norm_ffn1, w_ffn1_gate, w_ffn1_up, w_ffn1_down, norm_mix, w_in, cmp_pos_k, cmp_w1_k,
    cmp_w2_k, cmp_pos_v, cmp_w1_v, cmp_w2_v, w_out, norm_ffn2, w_ffn2_gate, w_ffn2_up,
    w_ffn2_down, rel_bias, norm_final, mem_2, ffn1_w_gate_2, ffn1_w_up_2, ffn1_w_down_2,
    ffn2_w_gate_2, ffn2_w_up_2, ffn2_w_down_2, ln_g_2, ln_b_2, w_out_2, w_mem_kv_2, rwkv_w_in_2,
    rwkv_mu_2, rwkv_w0_2, rwkv_w_up_2, rwkv_a0_2, rwkv_a_up_2, rwkv_g_up_2, rwkv_k_k_2,
    rwkv_k_a_2, rwkv_r_k_2, rwkv_lnx_g_2, rwkv_lnx_b_2, sb_w_in_2,
):
    x = first_block(
        x, norm_ffn1, w_ffn1_gate, w_ffn1_up, w_ffn1_down, norm_mix, w_in, cmp_pos_k, cmp_w1_k,
        cmp_w2_k, cmp_pos_v, cmp_w1_v, cmp_w2_v, w_out, norm_ffn2, w_ffn2_gate, w_ffn2_up,
        w_ffn2_down, rel_bias, norm_final,
    )
    return second_block(
        x, mem_2, ffn1_w_gate_2, ffn1_w_up_2, ffn1_w_down_2, ffn2_w_gate_2, ffn2_w_up_2,
        ffn2_w_down_2, ln_g_2, ln_b_2, w_out_2, w_mem_kv_2, rwkv_w_in_2, rwkv_mu_2, rwkv_w0_2,
        rwkv_w_up_2, rwkv_a0_2, rwkv_a_up_2, rwkv_g_up_2, rwkv_k_k_2, rwkv_k_a_2, rwkv_r_k_2,
        rwkv_lnx_g_2, rwkv_lnx_b_2, sb_w_in_2,
    )


_drawn_inputs = setup_inputs


def setup_inputs(seed=0):
    import zlib

    import numpy as np

    out = dict(_drawn_inputs(seed))
    spreads = {}
    factors = {'norm_mix': 2.929,
     'cmp_pos_k': 4.331,
     'norm_ffn2': 2.804,
     'rwkv_w_up_2': 8.0,
     'rwkv_k_k_2': 4.895,
     'rwkv_k_a_2': 2.915,
     'rwkv_lnx_g_2': 8.0,
     'rwkv_lnx_b_2': 8.0}
    for name, (base, spread) in spreads.items():
        noise = np.random.default_rng([zlib.crc32(name.encode()), seed]).standard_normal(out[name].shape)
        drawn = base * np.exp(spread * noise) if base else spread * noise
        out[name] = __import__('jax').numpy.asarray(drawn.astype(out[name].dtype))
    for name, factor in factors.items():
        out[name] = (out[name] * factor).astype(out[name].dtype)
    return out
```

```python
import math
from contextlib import ExitStack

import numpy as np

import concourse.bass as bass
from concourse import mybir

F32 = mybir.dt.float32
F32R = mybir.dt.float32r
ALU = mybir.AluOpType
ACT = mybir.ActivationFunctionType
AX = mybir.AxisListType

NT = 256
DM = 1024
NF = 22
NRAW = 4
NHL = 3
UW = 2048
BIG = 1e30
ALPHA = 4.0 ** 0.25
DECAY = math.exp(-0.5)

C_ID, C_TRI, C_KEEP, C_NEG, C_BLK, C_BLK2 = 0, 128, 256, 384, 512, 640
C_MLT, C_MLE, C_LEV, C_SCAN, C_I64, C_ONES, C_FLIP = 642, 706, 770, 1154, 1410, 1474, 1602
C_END = C_FLIP
V_MU, V_W0, V_A0, V_KK, V_KA, V_RK, V_PK, V_PV, V_END = 0, 20, 26, 32, 38, 44, 50, 66, 82


def unit_kinds():
    ffn = [True] * 33
    mixer1 = [True] * 12 + [False] * 4 + [True] * 4
    rwkv = [True] * 11 + [True] * 4
    sb = [True] * 10 + [True] * 4
    return ffn + mixer1 + ffn + [True] * 2 + ffn + rwkv + ffn + ffn + sb + ffn


class Queue:

    def __init__(self, engine, sem):
        self.engine, self.sem, self.n, self.seen, self.last = engine, sem, 0, {}, None

    def wait(self, *toks):
        for t in toks:
            if t is None:
                continue
            if isinstance(t, list):
                self.wait(*t)
                continue
            sem, value = t
            if self.seen.get(id(sem), 0) < value:
                self.seen[id(sem)] = value
                self.engine.wait_ge(sem, value)

    def __call__(self, fn, *toks):
        self.wait(*toks)
        self.n += 1
        fn(self.engine).then_inc(self.sem, 1)
        return (self.sem, self.n)

    def quiet(self, fn):
        self.last = fn(self.engine)

    def mark(self):
        self.n += 1
        self.last.then_inc(self.sem, 1)
        return (self.sem, self.n)


def program(nc, ctx, ws, cst, vec, base, relx, gains, x_in, mem_in, lora, gup, lnx, w2, out):
    def sb(name, shape, dt=F32):
        return ctx.enter_context(nc.sbuf_tensor(name, shape, dt))

    def sem(name):
        return ctx.enter_context(nc.semaphore(name))

    raw = [sb(f"raw{i}", [128, UW]) for i in range(NRAW)]
    whi = [sb(f"whi{i}", [128, UW], F32R) for i in range(NHL)]
    wlo = [sb(f"wlo{i}", [128, UW], F32R) for i in range(NHL)]
    x = sb("x", [128, 2, DM])
    xth = sb("xth", [128, 8, NT], F32R)
    xtl = sb("xtl", [128, 8, NT], F32R)
    hh = sb("hh", [128, 3, NT], F32R)
    hl = sb("hl", [128, 3, NT], F32R)
    gb = sb("gb", [128, 2, DM])
    cs = sb("cs", [128, C_END])
    vc = sb("vc", [128, V_END])
    sm = sb("sm", [128, 256])
    AR = sb("AR", [128, 20992])
    P = [ctx.enter_context(nc.psum_tensor(f"P{i}", [128, 512], F32)) for i in range(8)]

    T = Queue(nc.tensor, sem("s_T"))
    V = Queue(nc.vector, sem("s_V"))
    S = Queue(nc.scalar, sem("s_S"))
    G = Queue(nc.gpsimd, sem("s_G"))
    Y = Queue(nc.sync, sem("s_Y"))

    counts, sent = {}, {}

    def dma(q, o, i, s, *toks):
        q.wait(*toks)
        counts[id(s)] = counts.get(id(s), 0) + 16
        q.quiet(lambda e: e.dma_start(o, i).then_inc(s, 16))
        sent[id(s)] = (s, counts[id(s)])
        return sent[id(s)]

    s_raw = [sem(f"s_raw{i}") for i in range(NRAW)]
    s_cst, s_vec, s_x0, s_x1, s_gn, s_base, s_rel, s_mem = (sem(f"s_{n}") for n in (
        "cst", "vec", "x0", "x1", "gn", "base", "rel", "mem"))
    s_flip = sem("s_flip")
    s_dist = [sem(f"s_dist{i}") for i in range(2)]
    s_dup = [sem(f"s_dup{i}") for i in range(8)]
    s_lora, s_gup, s_lnx, s_w2, s_out = (sem(f"s_{n}") for n in ("lora", "gup", "lnx", "w2", "out"))

    ident = cs[:, C_ID:C_ID + 128]

    kinds = unit_kinds()
    nu = len(kinds)
    sidx = np.cumsum([0] + kinds)[:-1]
    t_load, t_hi, t_lo, t_done = {}, {}, {}, {}
    st = {"dma": 0, "split": 0, "take": 0}
    split_units = [u for u in range(nu) if kinds[u]]

    def pump():
        while st["dma"] < nu:
            u = st["dma"]
            old = u - NRAW
            if old >= 0:
                need = t_lo.get(old) if kinds[old] else t_done.get(old)
                if need is None:
                    return
            else:
                need = None
            t_load[u] = dma(Y, raw[u % NRAW][:, :], ws[u, :, :], s_raw[u % NRAW], need)
            st["dma"] += 1

    def split(v):
        while st["split"] <= v and st["split"] < nu:
            u = st["split"]
            st["split"] += 1
            if not kinds[u]:
                continue
            i = int(sidx[u])
            slot = i % NHL
            free = t_done[split_units[i - NHL]] if i >= NHL else None
            pump()
            r, h, l = raw[u % NRAW], whi[slot], wlo[slot]
            t_hi[u] = S(lambda e: e.activation(h[:, :], r[:, :], ACT.Copy), t_load[u], free)
            t_lo[u] = V(lambda e: e.tensor_tensor(l[:, :], r[:, :], h[:, :].bitcast(F32), ALU.subtract),
                        t_hi[u], t_load[u], free)
            pump()

    def take():
        u = st["take"]
        st["take"] += 1
        split(u)
        v = u
        while v + 1 < nu and v + 1 <= u + 2:
            j = v + 1
            if kinds[j]:
                i = int(sidx[j])
                if i >= NHL and split_units[i - NHL] not in t_done:
                    break
            v = j
        split(v)
        pump()
        if not kinds[u]:
            return u, raw[u % NRAW], None, t_load[u]
        slot = int(sidx[u]) % NHL
        return u, whi[slot], wlo[slot], t_lo[u]

    def done(u, tok):
        t_done[u] = tok
        pump()

    pf = [[] for _ in range(8)]
    ring = {"i": 0, "over": list(range(8))}

    def bank():
        ring["i"] += 1
        b = ring["over"][ring["i"] % len(ring["over"])]
        T.wait(*pf[b])
        pf[b] = []
        return b

    def mm(o, l, r, start=True, stop=True):
        T.quiet(lambda e: e.matmul(o, l, r, start=start, stop=stop, skip_group_check=True))

    def mm3(o, ah, al, bh, bl, start, stop):
        mm(o, ah, bh, start, False)
        mm(o, ah, bl, False, False)
        mm(o, al, bh, False, stop)

    def tr(o, i, n=128, base=0):
        T.quiet(lambda e: e.transpose(o, i, cs[base:base + n, C_ID + base:C_ID + base + n]))

    k_x = [dma(q, x[:, i, :], x_in[i * 128:(i + 1) * 128, :], s) for i, s, q in ((0, s_x0, Y), (1, s_x1, S))]
    k_vec = dma(G, vc[:, :], vec[:, :], s_vec)
    nrm = {"n": 0, "tok": None}

    def load_gains(rows, *toks, q=Y):
        t = None
        for j, r in enumerate(rows):
            src = bass.AP(gains.tensor, r * DM, [[0, 128], [1, DM]])
            if j == 0:
                t = dma(q, gb[:, 0, :], src, s_gn, *toks)
            else:
                t = dma(q, gb[:, 1, :], src, s_gn2, *toks)
        return [(s_gn, counts[id(s_gn)])] + ([(s_gn2, counts[id(s_gn2)])] if len(rows) > 1 else [])

    s_gn2 = sem("s_gn2")
    t_g = load_gains([0], q=S)
    k_cst = dma(S, cs[:, :], cst[:, 0:C_END], s_cst)

    XN = AR[:, 0:2048].rearrange("p (a n) -> p a n", a=2)
    SL = AR[:, 2048:2560].rearrange("p (a n) -> p a n", a=2)
    HF = AR[:, 2560:3072].rearrange("p (a n) -> p a n", a=2)

    def rms(t_x, t_gain, xn_free):
        toks = []
        for a in range(2):
            t1 = S(lambda e, a=a: e.activation(XN[:, a, :], x[:, a, :], ACT.Square, accum_out=sm[:, a:a + 1]),
                   t_x[a], xn_free)
            t2 = V(lambda e, a=a: e.tensor_scalar(sm[:, 2 + a:3 + a], sm[:, a:a + 1], 1.0 / DM, 1e-6, ALU.mult, ALU.add), t1)
            t3 = S(lambda e, a=a: e.activation(sm[:, 24 + a:25 + a], sm[:, 2 + a:3 + a], ACT.Sqrt), t2)
            t4 = V(lambda e, a=a: e.reciprocal(sm[:, 4 + a:5 + a], sm[:, 24 + a:25 + a]), t3)
            toks.append(V(lambda e, a=a: e.scalar_tensor_tensor(out=XN[:, a, :], in0=x[:, a, :], scalar=sm[:, 4 + a:5 + a],
                                                                in1=gb[:, 0, :], op0=ALU.mult, op1=ALU.mult), t4, t_gain, t1))
        return toks

    def layer_norm(t_x, t_gain):
        toks = []
        stt = sm[:, 8:20].rearrange("p (a n) -> p a n", a=2)
        for a in range(2):
            t0 = [V(lambda e, a=a, h=h: e.bn_stats(stt[:, h, :], x[:, a, h * 512:(h + 1) * 512]), t_x[a])
                  for h in range(2)]
            t1 = V(lambda e, a=a: e.bn_aggr(sm[:, 20 + 2 * a:22 + 2 * a], stt), *t0)
            t2 = V(lambda e, a=a: e.tensor_scalar(sm[:, 2 + a:3 + a], sm[:, 21 + 2 * a:22 + 2 * a], 1e-5, None, ALU.add), t1)
            t3 = S(lambda e, a=a: e.activation(sm[:, 24 + a:25 + a], sm[:, 2 + a:3 + a], ACT.Sqrt), t2)
            t4 = V(lambda e, a=a: e.scalar_tensor_tensor(out=x[:, a, :], in0=x[:, a, :], scalar=sm[:, 20 + 2 * a:21 + 2 * a],
                                                         in1=gb[:, 0, :], op0=ALU.subtract, op1=ALU.mult), t1, t_gain)
            t5 = V(lambda e, a=a: e.reciprocal(sm[:, 4 + a:5 + a], sm[:, 24 + a:25 + a]), t3)
            toks.append(V(lambda e, a=a: e.scalar_tensor_tensor(out=x[:, a, :], in0=x[:, a, :], scalar=sm[:, 4 + a:5 + a],
                                                                in1=gb[:, 1, :], op0=ALU.mult, op1=ALU.add), t4, t5))
        return toks

    xt = {"free": None}

    def turn(src, toks, banks=range(8), ks=range(8)):
        ready, banks, n, last = [], list(banks), 0, []
        ks = list(ks)
        for a in range(2):
            for g in range(0, len(ks), 4):
                kk = ks[g:g + 4]
                b = banks[n % len(banks)]
                n += 1
                T.wait(*pf[b], toks[a], k_cst)
                for j, k in enumerate(kk):
                    tr(P[b][:, j * 128:(j + 1) * 128], src(a, k))
                t0 = T.mark()
                last.append(t0)
                w = len(kk) * 128
                pv = P[b][:, 0:w].rearrange("p (k n) -> p k n", k=len(kk))
                oh = xth[:, kk[0]:kk[0] + len(kk), a * 128:(a + 1) * 128]
                ol = xtl[:, kk[0]:kk[0] + len(kk), a * 128:(a + 1) * 128]
                t1 = S(lambda e, pv=pv, oh=oh: e.activation(oh, pv, ACT.Copy), t0, xt["free"])
                t2 = V(lambda e, pv=pv, oh=oh, ol=ol: e.tensor_tensor(ol, pv, oh.bitcast(F32), ALU.subtract), t1, xt["free"])
                pf[b] = [t1, t2]
                ready += [t1, t2]
        return ready, last

    def tiles(t):
        return lambda a, k: t[:, a, k * 128:(k + 1) * 128]

    arena = {"free": []}

    def ffn(t_xt, filler=None):
        lo, sl_free, hf_free, hh_free = {}, {}, {}, {}
        first = {"v": True}

        def gate_up(f):
            u, wh, wl, tw = take()
            b = 4 + f % 3
            T.wait(tw, t_xt, *pf[b])
            for s in range(2):
                for k in range(8):
                    c = (s * 8 + k) * 128
                    mm3(P[b][:, s * NT:(s + 1) * NT], wh[:, c:c + 128], wl[:, c:c + 128],
                        xth[:, k, :], xtl[:, k, :], k == 0, k == 7)
            t = T.mark()
            done(u, t)
            i, j = f % 2, f % 3
            t1 = S(lambda e: e.activation(SL[:, i, :], P[b][:, 0:NT], ACT.Silu), t, sl_free.get(f - 2), arena["free"])
            t2 = V(lambda e: e.tensor_tensor(HF[:, i, :], P[b][:, NT:2 * NT], SL[:, i, :], ALU.mult), t1, hf_free.get(f - 2))
            sl_free[f] = t2
            pf[b] = [t1, t2]
            t3 = S(lambda e: e.activation(hh[:, j, :], HF[:, i, :], ACT.Copy), t2, hh_free.get(f - 3))
            t4 = V(lambda e: e.tensor_tensor(hl[:, j, :], HF[:, i, :], hh[:, j, :].bitcast(F32), ALU.subtract), t3)
            hf_free[f] = [t3, t4]
            lo[f] = t4
            return t

        def down(j):
            u, wh, wl, tw = take()
            T.wait(tw)
            for i in range(2):
                f = 2 * j + i
                T.wait(lo[f])
                for a in range(2):
                    for h in range(2):
                        if f == 0:
                            T.wait(*pf[2 * a + h])
                        c = i * DM + h * 512
                        mm3(P[2 * a + h][:, :], hh[:, f % 3, a * 128:(a + 1) * 128], hl[:, f % 3, a * 128:(a + 1) * 128],
                            wh[:, c:c + 512], wl[:, c:c + 512], f == 0, f == NF - 1)
                    if a == 0 and f == NF - 1:
                        ta = T.mark()
                t = T.mark()
                hh_free[f] = t
            done(u, t)
            return [ta if j == NF // 2 - 1 else t, t]

        gate_up(0)
        gate_up(1)
        for j in range(NF // 2):
            if j < NF // 2 - 1:
                gate_up(2 * j + 2)
            t = down(j)
            if j < NF // 2 - 1:
                tl = gate_up(2 * j + 3)
                if 2 * j + 3 == NF - 1:
                    xt["free"] = tl
            if filler is not None:
                filler(j)
        arena["free"] = []
        return t

    def residual(t_acc, scale):
        toks = []
        for a in range(2):
            r = []
            for h in range(2):
                xs = x[:, a, h * 512:(h + 1) * 512]
                t = V(lambda e, xs=xs, b=2 * a + h: e.scalar_tensor_tensor(out=xs, in0=P[b][:, :], scalar=scale, in1=xs,
                                                                          op0=ALU.mult, op1=ALU.add), t_acc[a], t_alpha["v"])
                pf[2 * a + h] = [t]
                r.append(t)
            toks.append(r)
        return toks

    t_alpha = {"v": None}

    def scale_x(*toks):
        t_alpha["v"] = [G(lambda e, a=a: e.tensor_scalar(x[:, a, :], x[:, a, :], ALPHA, None, ALU.mult), *toks)
                        for a in range(2)]

    def proj_cols(n_units, evac):
        for n in range(n_units):
            u, wh, wl, tw = take()
            b = bank()
            T.wait(tw)
            for s in range(2):
                for k in range(8):
                    c = (s * 8 + k) * 128
                    mm3(P[b][:, s * NT:(s + 1) * NT], wh[:, c:c + 128], wl[:, c:c + 128],
                        xth[:, k, :], xtl[:, k, :], k == 0, k == 7)
            t = T.mark()
            done(u, t)
            pf[b] = evac(n, b, t)

    def proj_rows(width, n_units, evac):
        bb = [bank(), bank()]
        per = 8 // n_units
        for n in range(n_units):
            u, wh, wl, tw = take()
            T.wait(tw)
            for k in range(per):
                kk = n * per + k
                for a in range(2):
                    mm3(P[bb[a]][:, 0:width], xth[:, kk, a * 128:(a + 1) * 128], xtl[:, kk, a * 128:(a + 1) * 128],
                        wh[:, k * width:(k + 1) * width], wl[:, k * width:(k + 1) * width], kk == 0, kk == 7)
            t = T.mark()
            done(u, t)
        for a in range(2):
            pf[bb[a]] = evac(a, bb[a], t)

    def out_proj(t_xt):
        for n in range(4):
            u, wh, wl, tw = take()
            T.wait(tw, t_xt)
            for i in range(2):
                k = 2 * n + i
                for a in range(2):
                    for h in range(2):
                        if k == 0:
                            T.wait(*pf[2 * a + h])
                        c = i * DM + h * 512
                        mm3(P[2 * a + h][:, :], xth[:, k, a * 128:(a + 1) * 128], xtl[:, k, a * 128:(a + 1) * 128],
                            wh[:, c:c + 512], wl[:, c:c + 512], k == 0, k == 7)
                    if a == 0 and k == 7:
                        ta = T.mark()
            t = T.mark()
            done(u, t)
        xt["free"] = t
        return [ta, t]

    def attend(units, L, Pr, Pt, mx, den, OB):
        n = len(units)
        tS, tE, tT, tC, tPV = {}, {}, {}, {}, {}
        sb_, pb_ = {}, {}
        rS = [b for b in ring["over"] if b not in OB]
        rs, rp = rS[:len(rS) // 2], rS[len(rS) // 2:]
        nL = len(L)

        def wd(u):
            return [(0, 128), (128, 256)] if u["bias"] is not None else [(0, 256), (256, 256)]

        def s0(i):
            u = units[i]
            b = rs[i % len(rs)]
            T.wait(*pf[b], u["need"])
            for a in range(2):
                o, w = wd(u)[a]
                mm(P[b][:, o:o + w], u["q"][:, a * 128:(a + 1) * 128], u["k"][:, 0:w])
            tS[i] = T.mark()
            sb_[i] = b

        def s1(i):
            u, b, r = units[i], sb_[i], i % nL
            ex, tm = [], []
            for a in range(2):
                o, w = wd(u)[a]
                m = mx[:, 4 * (i % 4) + a:4 * (i % 4) + a + 1]
                if u["bias"] is not None:
                    bi = u["bias"][:, 128:256] if a == 0 else u["bias"]
                    tm.append(V(lambda e, o=o, w=w, m=m, bi=bi: e.tensor_tensor_reduce(
                        L[r][:, o:o + w], P[b][:, o:o + w], bi, 1.0, -3e38, ALU.add, ALU.max, m), tS[i], tE.get(i - nL)))
                else:
                    tm.append(V(lambda e, o=o, w=w, m=m: e.tensor_reduce(m, P[b][:, o:o + w], AX.X, ALU.max), tS[i],
                                tE.get(i - 4)))
            nm = mx[:, 4 * (i % 4) + 2:4 * (i % 4) + 4]
            t = V(lambda e: e.tensor_scalar(nm, mx[:, 4 * (i % 4):4 * (i % 4) + 2], -1.0, None, ALU.mult), *tm)
            for a in range(2):
                o, w = wd(u)[a]
                src = L[r] if u["bias"] is not None else P[b]
                ex.append(S(lambda e, a=a, o=o, w=w, src=src: e.activation(
                    Pr[r][:, o:o + w], src[:, o:o + w], ACT.Exp, bias=nm[:, a:a + 1], scale=1.0,
                    accum_out=den[:, 2 * u["slot"] + a:2 * u["slot"] + a + 1]), t, tT.get(i - nL), *u.get("hold", [])))
            tE[i] = ex
            pf[b] = tm if u["bias"] is not None else ex

        def s2(i):
            u, r = units[i], i % nL
            b = rp[i % len(rp)]
            T.wait(*pf[b], tE[i])
            blocks = [0, 128, 256] if u["bias"] is not None else [0, 128, 256, 384]
            for j in blocks:
                tr(P[b][:, j:j + 128], Pr[r][:, j:j + 128])
            tT[i] = T.mark()
            w = blocks[-1] + 128
            q = V if i % 3 else S
            if q is V:
                tC[i] = V(lambda e: e.tensor_copy(Pt[r][:, 0:w], P[b][:, 0:w]), tT[i], tPV.get(i - nL))
            else:
                tC[i] = S(lambda e: e.activation(Pt[r][:, 0:w], P[b][:, 0:w], ACT.Copy), tT[i], tPV.get(i - nL))
            pf[b] = [tC[i]]

        def s3(i):
            u, r = units[i], i % nL
            T.wait(tC[i], u["needv"])
            c = u["col"]
            if i == 0:
                T.wait(*pf[OB[0]], *pf[OB[1]])
            if u["bias"] is not None:
                parts = [(0, [(0, 0)]), (1, [(128, 0), (256, 1)])]
            else:
                parts = [(0, [(0, 0), (128, 1)]), (1, [(256, 0), (384, 1)])]
            for a, lst in parts:
                for j, (o, s) in enumerate(lst):
                    mm(P[OB[a]][:, c:c + 64], Pt[r][:, o:o + 128], u["v"](s), j == 0, j == len(lst) - 1)
            tPV[i] = T.mark()

        for i in range(n + 2):
            if i < n:
                s0(i)
                s1(i)
            if 1 <= i <= n:
                s2(i - 1)
            if 2 <= i:
                s3(i - 2)
        return tPV[n - 1], [tE[i] for i in range(n)]

    def finish(tok):
        Y.wait(tok)

    BIAS = AR[:, 3072:7168].rearrange("p (h c) -> p h c", h=16)
    CB = AR[:, 20352:20592].rearrange("p (h a n) -> p h a n", h=8, a=2)
    HANK = AR[:, 7168:13312].rearrange("p (h c) -> p h c", h=16)
    BASE = AR[0:33, 13312:13824]
    RELX = AR[0:33, 13824:13840]
    VALS = AR[0:16, 13840:14352]
    FLIP = AR[:, 14352:14480]
    k_flip = dma(G, FLIP, cst[:, C_FLIP:C_FLIP + 128], s_flip)
    k_base = dma(G, BASE, base[:, :], s_base)
    k_rel = dma(G, RELX, relx[:, :], s_rel)

    t_xn = rms([k_x[0], k_x[1]], t_g, None)
    t_xt, t_tr = turn(tiles(XN), t_xn)

    b = bank()
    T.wait(k_base, k_rel)
    mm(P[b][0:16, :], RELX, BASE)
    t = T.mark()
    t1 = V(lambda e: e.tensor_copy(VALS, P[b][0:16, :]), t)
    pf[b] = [t1]
    dist = nc.dram_tensor("by_distance", (16, 512), F32).ap()
    t2 = dma(G, dist[:, :], VALS, s_dist[0], t1)
    k_hank = dma(G, HANK, bass.AP(dist.tensor, 0, [[1, 128], [512, 16], [1, 384]]), s_dist[1], t2)
    t_bias = []

    def bias_part(r):
        T.wait(k_hank, k_flip, *pf[7])
        if r < 8:
            mm(P[7][:, :], FLIP, HANK[:, 2 * r:2 * r + 2, 0:256])
            t = T.mark()
            t1 = S(lambda e: e.activation(BIAS[:, 2 * r:2 * r + 2, :], P[7][:, :].rearrange("p (h c) -> p h c", h=2),
                                          ACT.Copy), t)
        else:
            for a in range(2):
                c = 159 - 128 * a
                mm(P[7][:, a * 120:(a + 1) * 120], FLIP, HANK[:, 8:16, c:c + 225:16])
            t = T.mark()
            t1 = S(lambda e: e.activation(CB, P[7][:, 0:240].rearrange("p (a h n) -> p h a n", a=2, h=8), ACT.Copy), t)
        pf[7] = [t1]
        t_bias.append(t1)

    t_acc = ffn(t_xt, lambda j: bias_part(j - 2) if j > 1 else None)
    t_x = residual(t_acc, 0.5)
    t_g = load_gains([1], t_xn)
    t_xn = rms(t_x, t_g, t_tr)
    t_xt, t_tr = turn(tiles(XN), t_xn)

    def ar(a, n, s=None):
        v = AR[:, a:a + n]
        return v if s is None else v.rearrange(*s[0], **s[1])

    QA = ar(7168, 1024, (("p (j t) -> p j t",), dict(j=4)))
    KA = ar(8192, 1024, (("p (j t) -> p j t",), dict(j=4)))
    QB = ar(9216, 1024, (("p (j t) -> p j t",), dict(j=4)))
    KS2 = ar(10240, 512, (("p (g t) -> p g t",), dict(g=2)))
    KW2 = ar(10752, 512, (("p (g t) -> p g t",), dict(g=2)))
    VA = ar(11264, 1024, (("p (a c) -> p a c",), dict(a=2)))
    VG = ar(12288, 560, (("p (a c) -> p a c",), dict(a=2)))
    KV = ar(12848, 512, (("p (s t) -> p s t",), dict(s=2)))
    KSW = ar(13360, 512, (("p (s t) -> p s t",), dict(s=2)))
    X2 = ar(13872, 1024, (("p (s g t) -> p s g t",), dict(s=2, g=2)))
    BK = ar(14896, 960, (("p (s l g n) -> p s l g n",), dict(s=2, l=16, g=2)))
    LR = [ar(15856 + 384 * i, 384) for i in range(3)]
    PR = [ar(17008 + 384 * i, 384) for i in range(3)]
    PT = [ar(18160 + 384 * i, 384) for i in range(3)]
    HD = ar(19312, 120, (("p (s m n) -> p s m n",), dict(s=2, m=2)))
    KC2 = ar(19432, 30)
    VC = ar(19464, 128, (("p (g d) -> p g d",), dict(g=2)))
    W2 = ar(19592, 384)
    O = ar(0, 2048, (("p (a n) -> p a n",), dict(a=2)))
    CL = ar(2048, 240, (("p (h a n) -> p h a n",), dict(h=8, a=2)))
    CP = ar(2304, 240, (("p (h a n) -> p h a n",), dict(h=8, a=2)))
    CT = ar(13872, 2048)
    MX = sm[:, 32:48]
    DEN = sm[:, 48:112]
    GT = sm[:, 112:160]
    CMX = sm[:, 160:176]
    CDEN = sm[:, 176:192]
    RD = sm[:, 192:256]

    k_w2 = dma(G, W2, w2[:, :], s_w2)
    tq = {}

    def copy_to(dst, scale, key, w=2):
        def evac(n, b, t):
            o = dst[:, 2 * n:2 * n + 2, :]
            src = P[b][:, :].rearrange("p (s t) -> p s t", s=2)
            if n % 2 == 0:
                k = S(lambda e: e.activation(o, src, ACT.Copy, scale=scale), t)
            else:
                k = V(lambda e: e.tensor_scalar(o, src, scale, None, ALU.mult), t)
            tq.setdefault(key, []).append(k)
            return [k]
        return evac

    T.wait(t_xt)
    proj_cols(2, copy_to(QA, 0.125, "qa"))
    proj_cols(2, copy_to(KA, 1.0, "ka"))

    def evac_va(a, b, t):
        k = S(lambda e: e.activation(VA[:, a, :], P[b][:, :], ACT.Copy), t)
        tq.setdefault("va", []).append(k)
        return [k]
    proj_rows(512, 2, evac_va)
    proj_cols(2, copy_to(QB, 0.125, "qb"))
    proj_cols(1, copy_to(KV, 1.0, "kv"))
    proj_cols(1, copy_to(KSW, 1.0, "ksw"))

    def evac_vg(a, b, t):
        k = V(lambda e: e.tensor_copy(VG[:, a, 0:256], P[b][:, 0:256]), t)
        k2 = S(lambda e: e.activation(GT[:, a * 24:(a + 1) * 24], P[b][:, 256:280], ACT.Sigmoid), k)
        tq.setdefault("vg", []).extend([k, k2])
        return [k, k2]
    proj_rows(280, 2, evac_vg)
    xt["free"] = t_done[st["take"] - 1]

    dups = []
    for i, (dst, s) in enumerate(((KS2, 0), (KW2, 1))):
        t1 = dma(G, dst[64:128, 0, :], KSW[0:64, s, :], s_dup[2 * i], tq["ksw"])
        t2 = dma(G, dst[0:64, 1, :], KSW[64:128, s, :], s_dup[2 * i + 1], tq["ksw"])
        t3 = G(lambda e, dst=dst, s=s: e.tensor_copy(dst[0:64, 0, :], KSW[0:64, s, :]), tq["ksw"])
        t4 = G(lambda e, dst=dst, s=s: e.tensor_copy(dst[64:128, 1, :], KSW[64:128, s, :]), tq["ksw"])
        dups.append([t1, t2, t3, t4])
    xk = []
    for s in range(2):
        t1 = dma(G, X2[64:128, s, 0, 0:255], KV[0:64, s, 1:256], s_dup[4 + 2 * s], tq["kv"])
        t2 = dma(G, X2[0:64, s, 1, :], KV[64:128, s, :], s_dup[5 + 2 * s], tq["kv"])
        t3 = G(lambda e, s=s: e.tensor_copy(X2[0:64, s, 0, :], KV[0:64, s, :]), tq["kv"])
        t4 = G(lambda e, s=s: e.tensor_copy(X2[64:128, s, 1, 0:255], KV[64:128, s, 1:256]), tq["kv"])
        xk.append([t1, t2, t3, t4])

    t_bk = []
    for s in range(2):
        for g in range(2):
            base_ap = X2[:, s, g, :]
            src = bass.AP(base_ap.tensor, base_ap.offset, [list(base_ap.ap[0]), [2, 16], [16, 15]])
            pos = vc[:, V_PK + 16 * s:V_PK + 16 * s + 16].unsqueeze(2).to_broadcast([128, 16, 15])
            t_bk.append(V(lambda e, s=s, g=g, src=src, pos=pos: e.tensor_tensor(BK[:, s, :, g, :], src, pos, ALU.add),
                          xk[s], k_vec))
    t_hd = []
    for s in range(2):
        b0, b1 = bank(), bank()
        bb = [b0, b1]
        for half in range(2):
            u, w, _, tw = take()
            T.wait(tw, t_bk)
            for l in range(8):
                lp = half * 8 + l
                for m in range(2):
                    mm(P[bb[m]][:, 0:30], w[:, l * 256 + m * 128:l * 256 + m * 128 + 128],
                       BK[:, s, lp, :, :].rearrange("p g n -> p (g n)"), lp == 0, lp == 15)
            t = T.mark()
            done(u, t)
        for m in range(2):
            k = S(lambda e, s=s, m=m, b=bb[m]: e.activation(HD[:, s, m, :], P[b][:, 0:30], ACT.Silu), t)
            pf[bb[m]] = [k]
            t_hd.append(k)
    b = bank()
    T.wait(t_hd, k_w2)
    for m in range(2):
        mm(P[b][:, 0:30], W2[:, m * 128:(m + 1) * 128], HD[:, 0, m, :], m == 0, m == 1)
    for g in range(2):
        for m in range(2):
            mm(P[b][0:15, 64 + 64 * g:128 + 64 * g], HD[:, 1, m, g * 15:(g + 1) * 15],
               W2[:, 256 + m * 64:256 + (m + 1) * 64], m == 0, m == 1)
    t = T.mark()
    t1 = V(lambda e: e.tensor_copy(KC2, P[b][:, 0:30]), t)
    t2 = V(lambda e: e.tensor_copy(VC[0:15, :, :], P[b][0:15, 64:192].rearrange("p (g d) -> p g d", g=2)), t)
    pf[b] = [t1, t2]
    t_kc = [t1, t2]

    b2 = [bank(), bank()]
    T.wait(t_kc, tq["qb"])
    for h in range(8):
        o = 64 * (h % 2)
        for a in range(2):
            c = (h // 2 * 2 + a) * 15
            mm(P[b2[h % 2]][:, c:c + 15], QB[o:o + 64, h // 2, a * 128:(a + 1) * 128], KC2[o:o + 64, 15 * (h // 4):15 * (h // 4) + 15])
    t = T.mark()
    t1 = []
    for i in range(2):
        t1.append(V(lambda e: e.tensor_tensor(CL[:, i:8:2, :, :], P[b2[i]][:, 0:120].rearrange("p (h a n) -> p h a n", h=4, a=2),
                                              CB[:, i:8:2, :, :], ALU.add), t, t_bias, t_tr))
        pf[b2[i]] = [t1[-1]]
    CLv = CL.rearrange("p h a n -> p (h a) n")
    CPv = CP.rearrange("p h a n -> p (h a) n")
    t2 = V(lambda e: e.tensor_reduce(CMX, CLv, AX.X, ALU.max), t1)
    t3 = V(lambda e: e.tensor_scalar(CMX, CMX, -1e20, None, ALU.max), t2)
    t4 = V(lambda e: e.tensor_tensor(CLv, CLv, CMX.unsqueeze(2).to_broadcast([128, 16, 15]), ALU.subtract), t3)
    t5 = S(lambda e: e.activation(CPv, CLv, ACT.Exp), t4)
    t6 = V(lambda e: e.tensor_reduce(CDEN, CPv, AX.X, ALU.add), t5)
    t7 = V(lambda e: e.tensor_scalar(CDEN, CDEN, 1e-30, None, ALU.max), t6)
    t8 = V(lambda e: e.reciprocal(CDEN, CDEN), t7)
    GTv = GT.rearrange("p (a h c) -> p a h c", a=2, c=3)
    t9 = V(lambda e: e.tensor_tensor(CDEN.rearrange("p (h a) -> p a h", a=2), CDEN.rearrange("p (h a) -> p a h", a=2),
                                     GTv[:, :, :, 0], ALU.mult), t8, tq["vg"])
    t_ct = []
    for q4 in range(4):
        b = bank()
        T.wait(t5)
        for j in range(4):
            i = 4 * q4 + j
            tr(P[b][0:15, j * 128:(j + 1) * 128], CPv[:, i, :])
        t = T.mark()
        t_ct.append(S(lambda e, b=b, q4=q4: e.activation(CT[0:15, q4 * 512:(q4 + 1) * 512], P[b][0:15, :], ACT.Copy), t,
                      t_done[st["take"] - 1]))
        pf[b] = [t_ct[-1]]
    ob = [bank(), bank()]
    T.wait(t_ct, t_kc)
    for h in range(8):
        for a in range(2):
            i = 2 * h + a
            mm(P[ob[a]][:, h * 64:(h + 1) * 64], CT[0:15, i * 128:(i + 1) * 128], VC[0:15, h // 4, :])
    t = T.mark()
    t_o = []
    for a in range(2):
        cf = CDEN.rearrange("p (h a) -> p a h", a=2)[:, a, :].unsqueeze(2).to_broadcast([128, 8, 64])
        k = V(lambda e, a=a, cf=cf: e.tensor_tensor(O[:, a, 512:1024].rearrange("p (h d) -> p h d", h=8),
                                                    P[ob[a]][:, :].rearrange("p (h d) -> p h d", h=8), cf, ALU.mult), t, t9, t_tr)
        pf[ob[a]] = [k]
        t_o.append(k)

    def heads(which):
        us = []
        for h in range(8):
            o, j, g = 64 * (h % 2), h // 2, h // 4
            if which == 0:
                u = dict(q=QA[o:o + 64, j, :], k=KA[o:o + 64, j, :], v=lambda s, h=h: VA[:, s, h * 64:(h + 1) * 64],
                         bias=BIAS[:, h, :], need=[tq["qa"], tq["ka"], t_bias], needv=tq["va"])
            else:
                kk = (KS2, KW2)[which - 1]
                u = dict(q=QB[o:o + 64, j, :], k=kk[o:o + 64, g, :],
                         v=lambda s, g=g: VG[:, s, (which - 1) * 128 + g * 64:(which - 1) * 128 + g * 64 + 64],
                         bias=BIAS[:, 8 + h, :], need=[tq["qb"], dups[which - 1]], needv=tq["vg"])
            u.update(col=h * 64, slot=8 * which + h)
            us.append(u)
        return us

    TM = ar(2560, 512)
    t_prev = t_o
    for which in range(3):
        OB = [(6, 7), (4, 5)][which % 2]
        tpv, tes = attend(heads(which), LR, PR, PT, MX, DEN, OB)
        dn = DEN[:, 16 * which:16 * which + 16]
        rd = RD[:, 16 * which:16 * which + 16]
        k1 = V(lambda e: e.reciprocal(rd, dn), tes)
        rv = rd.rearrange("p (h a) -> p a h", a=2)
        if which:
            k1 = V(lambda e: e.tensor_tensor(rv, rv, GTv[:, :, :, which], ALU.mult), k1)
        nt = []
        for a in range(2):
            cf = rv[:, a, :].unsqueeze(2).to_broadcast([128, 8, 64])
            src = P[OB[a]][:, :].rearrange("p (h d) -> p h d", h=8)
            if which == 0:
                k = V(lambda e, a=a, cf=cf, src=src: e.tensor_tensor(O[:, a, 0:512].rearrange("p (h d) -> p h d", h=8),
                                                                     src, cf, ALU.mult), k1, tpv, t_tr)
                nt.append(k)
            else:
                k = V(lambda e, cf=cf, src=src: e.tensor_tensor(TM.rearrange("p (h d) -> p h d", h=8), src, cf, ALU.mult),
                      k1, tpv, t_prev, nt)
                nt.append(V(lambda e, a=a: e.tensor_tensor(O[:, a, 512:1024], O[:, a, 512:1024], TM, ALU.add), k))
            pf[OB[a]] = [k]
        if which == 0:
            t_om = nt
        else:
            t_prev = nt
    t_xt, t_tr = turn(tiles(O), [[t_om[0], t_prev[0]], [t_om[1], t_prev[1]]])
    t_acc = out_proj(t_xt)
    t_x = residual(t_acc, 1.0)
    arena["free"] = [t_tr]
    t_g = load_gains([2], t_xn)
    t_xn = rms(t_x, t_g, t_tr)
    t_xt, t_tr = turn(tiles(XN), t_xn)
    t_acc = ffn(t_xt)
    t_x = residual(t_acc, 0.5)

    t_g = load_gains([3], t_xn)
    t_xn = rms(t_x, t_g, t_tr)
    t_x = [S(lambda e, a=a: e.activation(x[:, a, :], XN[:, a, :], ACT.Copy), t_xn[a]) for a in range(2)]
    t_xcopy = t_x

    MK = ar(19968, 512, (("p (j m) -> p j m",), dict(j=2)))
    MV = ar(20480, 512, (("p (a c) -> p a c",), dict(a=2)))
    MEM = ar(3072, 2048, (("p (a n) -> p a n",), dict(a=2)))
    k_mem = dma(G, MEM, mem_in.rearrange("(a p) n -> p a n", p=128), s_mem, t_om, t_acc)
    t_mt, _ = turn(tiles(MEM), [k_mem, k_mem])
    T.wait(t_mt)
    proj_cols(1, lambda n, b, t: tq.setdefault("mk", [S(lambda e: e.activation(
        MK, P[b][:, :].rearrange("p (j m) -> p j m", j=2), ACT.Copy), t)]))
    proj_rows(256, 1, lambda a, b, t: [tq.setdefault(f"mv{a}", S(lambda e: e.activation(
        MV[:, a, :], P[b][:, 0:256], ACT.Copy), t))])
    xt["free"] = t_done[st["take"] - 1]
    t_xt, t_tr = turn(tiles(x), t_x)
    scale_x(t_tr)
    arena["free"] = [t_x, t_tr]

    def norm_step(t_acc, scale, rows, free):
        t_x = residual(t_acc, scale)
        t_g = load_gains(rows, free)
        t_x = layer_norm(t_x, t_g)
        return t_x

    def mem_attention(MQ, t_mq, ocols, Lb, t_free):
        PRm = [Lb[:, 512 * i:512 * (i + 1)] for i in range(3)]
        PTm = [Lb[:, 1536 + 512 * i:1536 + 512 * (i + 1)] for i in range(3)]
        us = []
        for h in range(4):
            o = 64 * (h % 2)
            us.append(dict(q=MQ[o:o + 64, h // 2, :], k=MK[o:o + 64, h // 2, :],
                           v=lambda s, h=h: MV[:, s, h * 64:(h + 1) * 64], bias=None,
                           need=[t_mq, tq["mk"]], needv=[tq["mv0"], tq["mv1"]], col=h * 64, slot=h, hold=[t_free]))
        tpv, tes = attend(us, PRm, PRm, PTm, MX, DEN, (6, 7))
        k1 = V(lambda e: e.reciprocal(RD[:, 0:8], DEN[:, 0:8]), tes)
        nt = []
        for a in range(2):
            cf = RD[:, 0:8].rearrange("p (h a) -> p a h", a=2)[:, a, :].unsqueeze(2).to_broadcast([128, 4, 64])
            k = V(lambda e, a=a, cf=cf: e.tensor_tensor(ocols[a].rearrange("p (h d) -> p h d", h=4),
                                                        P[6 + a][:, 0:256].rearrange("p (h d) -> p h d", h=4), cf, ALU.mult),
                  k1, tpv, t_free)
            pf[6 + a] = [k]
            nt.append(k)
        return nt

    t_acc = ffn(t_xt)
    t_x = norm_step(t_acc, 0.5, [4, 5], t_xn)
    t_xt, t_tr = turn(tiles(x), t_x)
    scale_x(t_tr)

    SL_ = [ar(1536 * i, 1536) for i in range(13)]

    def pairs(t):
        return t.rearrange("p (j t) -> p j t", j=6)

    def rows(t):
        return t.rearrange("p (a n) -> p a n", a=2)

    gflat = gb[:, :, :].rearrange("p a n -> p (a n)")
    GUP, LORA, MQ = gflat[:, 0:768], gflat[:, 768:1536], gflat[:, 1536:2048].rearrange("p (j t) -> p j t", j=2)
    k_gup = dma(G, GUP, gup[:, :], s_gup, t_x)
    k_lora = dma(G, LORA, lora[:, :], s_lora, t_x)
    R, K, VT = pairs(SL_[0]), pairs(SL_[1]), pairs(SL_[7])
    LT = SL_[10].rearrange("p (j t) -> p j t", j=6)
    OM = sm[:, 192:212]
    OKA = sm[:, 212:218]
    WL = sm[:, 112:136]
    BON = sm[:, 136:160]
    t_om = G(lambda e: e.tensor_scalar(OM, vc[:, V_MU:V_MU + 20], -1.0, 1.0, ALU.mult, ALU.add), t_x, k_vec)
    t_oka = G(lambda e: e.tensor_scalar(OKA, vc[:, V_KA:V_KA + 6], -1.0, 1.0, ALU.mult, ALU.add), t_x, k_vec)
    tz = {}

    def shifted(dst, first, n, b, t):
        last, first_ = [], []
        for s in range(2):
            i = 2 * n + s
            d = dst[:, i, :]
            src = P[b][:, s * NT:(s + 1) * NT]
            om = OM[:, first + i:first + i + 1]
            first_.append(S(lambda e: e.activation(d, src, ACT.Copy, scale=om), t, t_om, t_acc))
        for s in range(2):
            i = 2 * n + s
            d = dst[:, i, :]
            src = P[b][:, s * NT:(s + 1) * NT]
            m = vc[:, V_MU + first + i:V_MU + first + i + 1]
            last.append(V(lambda e, d=d, src=src, m=m: e.scalar_tensor_tensor(
                out=d[:, 1:NT], in0=src[:, 0:NT - 1], scalar=m, in1=d[:, 1:NT], op0=ALU.mult, op1=ALU.add), *first_))
            tz[first + i] = last[-1]
        return last

    T.wait(t_xt)
    proj_cols(3, lambda n, b, t: shifted(R, 0, n, b, t))
    proj_cols(3, lambda n, b, t: shifted(K, 6, n, b, t))
    proj_cols(3, lambda n, b, t: shifted(VT, 12, n, b, t))
    proj_cols(1, lambda n, b, t: shifted(LT, 18, n, b, t))

    def evac_mq(n, b, t):
        tq["mq"] = [S(lambda e: e.activation(MQ, P[b][:, :].rearrange("p (j t) -> p j t", j=2), ACT.Copy, scale=0.125), t, t_x)]
        return tq["mq"]
    proj_cols(1, evac_mq)
    xt["free"] = t_done[st["take"] - 1]
    t_r, t_k = [tz[i] for i in range(6)], [tz[i] for i in range(6, 12)]

    t_th = S(lambda e: e.activation(LT[0:64, 0, :], LT[0:64, 0, :], ACT.Tanh), tz[18])
    t_dg = S(lambda e: e.activation(LT[:, 1, :], LT[:, 1, :], ACT.Sigmoid), tz[19])
    LD, A, Cc, KK, TP = (pairs(SL_[i]) for i in (3, 4, 5, 6, 11))
    SQ = pairs(SL_[12])
    t_ld, t_a, t_c = [], [], []
    for j in range(6):
        b, b2 = bank(), bank()
        T.wait(t_th, tz[18], k_lora)
        mm(P[b][:, 0:NT], LORA[0:64, j * 128:(j + 1) * 128], LT[0:64, 0, :])
        mm(P[b2][:, 0:NT], LORA[64:128, j * 128:(j + 1) * 128], LT[64:128, 0, :])
        t = T.mark()
        t1 = S(lambda e, b=b, j=j: e.activation(LD[:, j, :], P[b][:, 0:NT], ACT.Sigmoid, bias=vc[:, V_W0 + j:V_W0 + j + 1]), t)
        t2 = S(lambda e, j=j: e.activation(A[:, j, :], P[b2][:, 0:NT], ACT.Sigmoid, bias=vc[:, V_A0 + j:V_A0 + j + 1]), t)
        pf[b], pf[b2] = [t1], [t2]
        t_ld.append(G(lambda e, j=j: e.tensor_scalar(LD[:, j, :], LD[:, j, :], -DECAY, None, ALU.mult), t1))
        t_a.append(t2)
    DGK = gflat[:, 768:1024]
    t_lora = t
    t_dg2 = S(lambda e: e.activation(DGK, LT[:, 1, :], ACT.Copy), t_dg, t_lora)
    t_kx, t_sq, t_rn = [], [], []
    for j in range(6):
        kk_ = vc[:, V_KK + j:V_KK + j + 1]
        t_kx.append(V(lambda e, j=j, kk_=kk_: e.tensor_scalar(KK[:, j, :], K[:, j, :], kk_, None, ALU.mult), tz[6 + j]))
        t_sq.append(S(lambda e, j=j: e.activation(SQ[:, j, :], KK[:, j, :], ACT.Square), t_kx[-1]))
    for n in range(3):
        b = bank()
        T.wait(t_sq[2 * n + 1], k_cst)
        mm(P[b][:, :], cs[:, C_BLK:C_BLK + 128], SQ[:, 2 * n:2 * n + 2, :].rearrange("p j t -> p (j t)"))
        t = T.mark()
        tp = TP[:, 2 * n:2 * n + 2, :].rearrange("p j t -> p (j t)")
        t1 = V(lambda e, b=b, tp=tp: e.tensor_scalar(tp, P[b][:, :], 1e-24, None, ALU.max), t)
        pf[b] = [t1]
        t2 = S(lambda e, tp=tp: e.activation(tp, tp, ACT.Sqrt), t1)
        t3 = V(lambda e, tp=tp: e.reciprocal(tp, tp), t2)
        kk2 = KK[:, 2 * n:2 * n + 2, :].rearrange("p j t -> p (j t)")
        t_rn.append(V(lambda e, tp=tp, kk2=kk2: e.tensor_tensor(kk2, kk2, tp, ALU.mult), t3))
    Vt = rows(SL_[2])

    def by_tokens(src, dst, toks, free=None):
        res = []
        for a in range(2):
            for lo_, w in ((0, 4), (4, 2)):
                b = bank()
                T.wait(*toks)
                for j in range(w):
                    tr(P[b][:, j * 128:(j + 1) * 128], src[:, lo_ + j, a * 128:(a + 1) * 128])
                t = T.mark()
                o, i = dst[:, a, lo_ * 128:(lo_ + w) * 128], P[b][:, 0:w * 128]
                if w == 4:
                    k = S(lambda e, o=o, i=i: e.activation(o, i, ACT.Copy), t, free)
                else:
                    k = V(lambda e, o=o, i=i: e.tensor_copy(o, i), t, free)
                pf[b] = [k]
                res.append(k)
        return res, t

    t_vt, t_vtp = by_tokens(VT, Vt, [tz[12 + j] for j in range(6)])
    for j in range(6):
        ka, ok = vc[:, V_KA + j:V_KA + j + 1], OKA[:, j:j + 1]
        rk = vc[:, V_RK + j:V_RK + j + 1]
        t_c.append(V(lambda e, j=j: e.tensor_tensor_scan(Cc[:, j, :], cs[:, C_SCAN:C_SCAN + NT], LD[:, j, :], 0.0,
                                                         ALU.mult, ALU.add), t_ld[j], k_cst))
        t1 = V(lambda e, j=j, ka=ka, ok=ok: e.tensor_scalar(TP[:, j, :], A[:, j, :], ka, ok, ALU.mult, ALU.add), t_a[j], t_oka, t_rn)
        t2 = V(lambda e, j=j: e.tensor_tensor(K[:, j, :], K[:, j, :], TP[:, j, :], ALU.mult), t1)
        t3 = V(lambda e, j=j, rk=rk: e.scalar_tensor_tensor(out=SQ[:, j, :], in0=R[:, j, :], scalar=rk, in1=K[:, j, :],
                                                            op0=ALU.mult, op1=ALU.mult), t2, tz[j], t_rn)
        t4 = G(lambda e, j=j: e.tensor_tensor(A[:, j, :], A[:, j, :], KK[:, j, :], ALU.mult), t1, t_rn)
        t_k[j], t_sq[j], t_a[j] = t2, t3, t4
    b = bank()
    T.wait(t_sq)
    for a in range(2):
        for j in range(6):
            c = a * 12 + 2 * j
            mm(P[b][:, c:c + 2], SQ[:, j, a * 128:(a + 1) * 128], cs[:, C_BLK2:C_BLK2 + 2])
    t = T.mark()
    t_bon = V(lambda e: e.tensor_copy(BON, P[b][:, 0:24]), t)
    pf[b] = [t_bon]
    t_bonp = t
    KR = AR[:, 8 * 1536:10 * 1536].rearrange("p (j c s t) -> p j c s t", j=6, c=4, s=2)

    def ch(t):
        return t.rearrange("p (c t) -> p c t", c=4)

    t_mat, t_kr = [], []
    for j in range(6):
        t1 = S(lambda e, j=j: e.activation(TP[:, j, :], Cc[:, j, :], ACT.Exp, scale=-1.0), t_c[j], t_k[j])
        t2 = V(lambda e, j=j: e.tensor_tensor(A[:, j, :], A[:, j, :], TP[:, j, :], ALU.mult), t1, t_a[j])
        t3 = V(lambda e, j=j: e.tensor_tensor(K[:, j, :], K[:, j, :], TP[:, j, :], ALU.mult), t1, t_k[j], t_sq[j])
        t4 = G(lambda e, j=j: e.tensor_tensor(LD[:, j, :], Cc[:, j, :], LD[:, j, :], ALU.subtract), t_c[j])
        t5 = S(lambda e, j=j: e.activation(Cc[:, j, :], Cc[:, j, :], ACT.Exp), t1, t4)
        t6 = S(lambda e, j=j: e.activation(LD[:, j, :], LD[:, j, :], ACT.Exp), t4)
        t7 = V(lambda e, j=j: e.tensor_tensor(KR[:, j, :, 1, :], ch(R[:, j, :]), ch(Cc[:, j, :]), ALU.mult), t5, t_r[j])
        t8 = V(lambda e, j=j: e.tensor_tensor(KR[:, j, :, 0, :], ch(KK[:, j, :]), ch(LD[:, j, :]), ALU.mult), t6, t_rn)
        t9 = G(lambda e, j=j: e.tensor_copy(WL[:, 4 * j:4 * j + 4], Cc[:, j, 63:NT:64]), t5)
        t_mat.append([t2, t3])
        t_kr.append([t7, t8, t9])

    def blocks(t):
        return t.rearrange("p (q h t) -> p q h t", q=2, h=12)

    AT, CT_, RBT, RKT, X, XT, T1, AM = (blocks(SL_[i]) for i in (5, 6, 7, 12, 10, 11, 4, 1))
    def flat(t):
        return t.rearrange("p q h t -> p (q h) t")

    t_at, t_ct, t_rb, t_rk = {}, {}, {}, {}
    for g in range(3):
        for what in range(2):
            for hb in range(2):
                src, d0, d1 = ((A, AT, RBT), (K, CT_, RKT))[what]
                b = bank()
                T.wait(t_mat, t_kr, t_vtp, t_bonp)
                o = 64 * hb
                for i in range(4):
                    q, j = divmod(4 * g + i, 6)
                    for p in range(2):
                        c = 2 * q + p
                        mm(P[b][64 * p:64 * p + 64, i * 128:(i + 1) * 128], src[o:o + 64, j, c * 64:(c + 1) * 64],
                           KR[o:o + 64, j, c, :, :].rearrange("p s t -> p (s t)"))
                t = T.mark()
                pv = P[b][:, :].rearrange("p (h s t) -> p h s t", h=4, s=2)
                m0 = cs[:, C_MLT:C_MLT + 64].unsqueeze(1).to_broadcast([128, 4, 64])
                m1 = cs[:, C_MLE:C_MLE + 64].unsqueeze(1).to_broadcast([128, 4, 64])
                at_ = slice(8 * g + hb, 8 * g + 8, 2)
                t1 = V(lambda e: e.tensor_tensor(flat(d0)[:, at_, :], pv[:, :, 0, :], m0, ALU.mult), t, t_kr, t_dg2)
                t2 = V(lambda e: e.tensor_tensor(flat(d1)[:, at_, :], pv[:, :, 1, :], m1, ALU.mult), t, t_kr)
                pf[b] = [t1, t2]
                (t_at, t_ct)[what][(g, hb)] = t1
                (t_rb, t_rk)[what][(g, hb)] = t2
    t_prod = t
    Bt, Kt = rows(SL_[0]), rows(SL_[3])
    t_bt, _ = by_tokens(A, Bt, [t_mat[j][0] for j in range(6)], t_kr)
    t_kt, t_turned = by_tokens(K, Kt, [t_mat[j][1] for j in range(6)], t_kr)
    fAT, fX, fXT, fT1, fAM = (flat(t) for t in (AT, X, XT, T1, AM))
    i64 = cs[:, C_I64:C_I64 + 64].unsqueeze(1).to_broadcast([128, 8, 64])
    t_all_at = list(t_at.values())
    tx, txt, tam, tam_free = {}, {}, {}, {}
    gs = [slice(8 * g, 8 * g + 8) for g in range(3)]

    def level_mask(l, g):
        m = cs[:, C_LEV + 64 * l:C_LEV + 64 * l + 64].unsqueeze(1).to_broadcast([128, 8, 64])
        tam[g] = G(lambda e: e.tensor_tensor(fAM[:, gs[g], :], fAT[:, gs[g], :], m, ALU.mult),
                   t_all_at, t_turned, t_prod, tam_free.get(g), t_bonp)

    def group_mm(b, g, l, r):
        for i in range(8):
            for p in range(2):
                mm(P[b][64 * p:64 * p + 64, i * 64:(i + 1) * 64], l[64 * p:64 * p + 64, 8 * g + i, :], r(p, i))

    for g in range(3):
        level_mask(0, g)
        txt[g] = V(lambda e, g=g: e.tensor_tensor(fXT[:, gs[g], :], i64, fAM[:, gs[g], :], ALU.subtract), tam[g], t_mat)
    for g in range(3):
        b = bank()
        T.wait(tam[g])
        group_mm(b, g, fAM, lambda p, i: cs[64 * p:64 * p + 64, C_I64:C_I64 + 64])
        t = T.mark()
        tx[g] = V(lambda e, g=g, b=b: e.tensor_tensor(fX[:, gs[g], :], i64, P[b][:, :].rearrange("p (i t) -> p i t", i=8),
                                                      ALU.subtract), t, t_dg2)
        pf[b] = [tx[g]]
        tam_free[g] = [t, txt[g]]
    for l in range(1, 6):
        t1s = {}
        for g in range(3):
            level_mask(l, g)
        for g in range(3):
            b = bank()
            T.wait(tam[g], tx[g])
            group_mm(b, g, fAM, lambda p, i, g=g: fX[64 * p:64 * p + 64, 8 * g + i, :])
            t = T.mark()
            tam_free[g] = t
            t1s[g] = S(lambda e, g=g, b=b: e.activation(fT1[:, gs[g], :], P[b][:, :].rearrange("p (i t) -> p i t", i=8),
                                                        ACT.Copy), t, t_turned, t_prod, txt[g])
            pf[b] = [t1s[g]]
        for g in range(3):
            T.wait(t1s[g], txt[g])
            ps = []
            if l < 5:
                b = bank()
                group_mm(b, g, fXT, lambda p, i, g=g: fT1[64 * p:64 * p + 64, 8 * g + i, :])
                ps.append(b)
            b3 = bank()
            group_mm(b3, g, fT1, lambda p, i, g=g: fXT[64 * p:64 * p + 64, 8 * g + i, :])
            t = T.mark()
            if ps:
                tx[g] = V(lambda e, g=g, b=ps[0]: e.tensor_tensor(fX[:, gs[g], :], fX[:, gs[g], :],
                                                                  P[b][:, :].rearrange("p (i t) -> p i t", i=8),
                                                                  ALU.subtract), t)
                pf[ps[0]] = [tx[g]]
            txt[g] = V(lambda e, g=g, b=b3: e.tensor_tensor(fXT[:, gs[g], :], fXT[:, gs[g], :],
                                                            P[b][:, :].rearrange("p (i t) -> p i t", i=8),
                                                            ALU.subtract), t)
            pf[b3] = [txt[g]]
    t_inv = list(txt.values())
    t_invp = t
    RH, UU = SL_[4][:, 0:768], SL_[4][:, 768:1536]
    STT = [SL_[1][:, 384 * i:384 * (i + 1)].rearrange("p (j n) -> p j n", j=6) for i in range(2)]
    STM = SL_[1][:, 768:1152].rearrange("p (j n) -> p j n", j=6)
    OUT = rows(SL_[10])
    CV, GK = rows(SL_[5]), rows(SL_[6])
    WLv = WL.rearrange("p (j c) -> p j c", j=6)

    def heads_of(bb, o):
        return lambda h: P[bb[h // 8]][o:o + 64, (h % 8) * 64:(h % 8) * 64 + 64]

    def parity(bb, o):
        return lambda h: P[bb[h % 2]][o:o + 64, (h // 2) * 64:(h // 2) * 64 + 64]

    def of_parity(t, i):
        return t.rearrange("p (j b d) -> p j b d", j=6, b=2)[:, :, i, :]

    def head_cols(t, h):
        return t[:, h * 64:(h + 1) * 64]

    def six(b, o):
        return P[b][o:o + 64, 0:384].rearrange("p (j d) -> p j d", j=6)

    t_cv = []
    for q in range(2):
        bb = [bank(), bank()]
        T.wait(list(t_ct.values()), t_vt)
        for h in range(12):
            for o in (0, 64):
                mm(heads_of(bb, o)(h), CT_[o:o + 64, q, h, :], head_cols(Vt[o:o + 64, q, :], h))
        t = T.mark()
        for i, (lo_, w) in enumerate(((0, 512), (512, 256))):
            k = S(lambda e: e.activation(CV[:, q, lo_:lo_ + w], P[bb[i]][:, 0:w], ACT.Copy, scale=-1.0), t, list(tam.values()))
            pf[bb[i]] = [k]
            t_cv.append(k)
    t_cvp = t
    t_st, t_or = None, []
    need0 = [t_inv, list(t_rb.values()), list(t_rk.values()), t_bt, t_kt, t_vt]
    for c in range(4):
        q, p = c // 2, c % 2
        o = 64 * p
        sc, sn = STT[c % 2], STT[(c + 1) % 2]
        cv = CV[o:o + 64, q, :]
        T.wait(need0)
        if c:
            bb = [bank(), bank()]
            T.wait(t_st)
            for h in range(12):
                ho, j = 64 * (h % 2), h // 2
                mm(parity(bb, o)(h), KR[ho:ho + 64, j, c, 0, :], sc[ho:ho + 64, j, :])
            t = T.mark()
            t1 = []
            for i in range(2):
                k = V(lambda e: e.tensor_tensor(of_parity(RH[o:o + 64, :], i), of_parity(cv, i), six(bb[i], o), ALU.subtract),
                      t, t_cv, t_invp)
                pf[bb[i]] = [k]
                t1.append(k)
            rh = RH[o:o + 64, :]
        else:
            t1, rh = t_cv, cv
        bb = [bank(), bank()]
        T.wait(t1)
        for h in range(12):
            mm(heads_of(bb, o)(h), XT[o:o + 64, q, h, :], head_cols(rh, h))
        t = T.mark()
        uu = UU[o:o + 64, :]
        t1 = V(lambda e: e.tensor_copy(uu[:, 0:512], P[bb[0]][o:o + 64, :]), t, t_invp)
        t2 = S(lambda e: e.activation(uu[:, 512:768], P[bb[1]][o:o + 64, 0:256], ACT.Copy), t, t_invp)
        pf[bb[0]], pf[bb[1]] = [t1], [t2]
        T.wait(t1, t2)
        vt = Vt[o:o + 64, q, :]
        if c < 3:
            b = bank()
            for h in range(12):
                ho, j = 64 * (h % 2), h // 2
                d = P[b][ho:ho + 64, j * 64:(j + 1) * 64]
                mm(d, head_cols(Bt[o:o + 64, q, :], h), head_cols(uu, h), True, False)
                mm(d, head_cols(Kt[o:o + 64, q, :], h), head_cols(vt, h), False, True)
            t = T.mark()
            wl = WLv[:, :, c].unsqueeze(2).to_broadcast([128, 6, 64])
            pv = P[b][:, 0:384].rearrange("p (j n) -> p j n", j=6)
            if c:
                t3 = V(lambda e: e.tensor_tensor(STM, pv, sc, ALU.add), t, t_st)
                t_st = V(lambda e: e.tensor_tensor(sn, STM, wl, ALU.mult), t3, t_or)
            else:
                t3 = t_st = V(lambda e: e.tensor_tensor(sn, pv, wl, ALU.mult), t, t_invp)
            pf[b] = [t3]
        bb = [bank(), bank()]
        for h in range(12):
            d = heads_of(bb, o)(h)
            mm(d, RBT[o:o + 64, q, h, :], head_cols(uu, h), True, False)
            mm(d, RKT[o:o + 64, q, h, :], head_cols(vt, h), False, True)
        t = T.mark()
        ot = OUT[o:o + 64, q, :]
        t1 = S(lambda e: e.activation(ot[:, 0:512], P[bb[0]][o:o + 64, :], ACT.Copy), t, t_invp)
        t2 = S(lambda e: e.activation(ot[:, 512:768], P[bb[1]][o:o + 64, 0:256], ACT.Copy), t, t_invp)
        pf[bb[0]], pf[bb[1]] = [t1], [t2]
        res = [t1, t2]
        if c:
            bb = [bank(), bank()]
            for h in range(12):
                ho, j = 64 * (h % 2), h // 2
                mm(parity(bb, o)(h), KR[ho:ho + 64, j, c, 1, :], sc[ho:ho + 64, j, :])
            t = T.mark()
            for i in range(2):
                k = V(lambda e: e.tensor_tensor(of_parity(ot, i), of_parity(ot, i), six(bb[i], o), ALU.add), t, t1, t2)
                pf[bb[i]] = [k]
                res.append(k)
        t_or = [t]
        tq.setdefault("out", []).extend(res)
    t_gk = []
    for a in range(2):
        bb = [bank(), bank()]
        T.wait(t_dg2, k_gup)
        mm(P[bb[0]][:, :], DGK[:, a * 128:(a + 1) * 128], GUP[:, 0:512])
        mm(P[bb[1]][:, 0:256], DGK[:, a * 128:(a + 1) * 128], GUP[:, 512:768])
        t = T.mark()
        k1 = S(lambda e, a=a, bb=bb: e.activation(GK[:, a, 0:512], P[bb[0]][:, :], ACT.Copy), t, t_cvp)
        k2 = V(lambda e, a=a, bb=bb: e.tensor_copy(GK[:, a, 512:768], P[bb[1]][:, 0:256]), t, t_cvp)
        pf[bb[0]], pf[bb[1]] = [k1], [k2]
        t_gk += [k1, k2]
    t_gp = t
    t_memo = mem_attention(MQ, tq["mq"], [gflat[:, 1536:1792], gflat[:, 1792:2048]], AR[:, 11 * 1536:13 * 1536], [t_gp])
    k_lnx = dma(G, gflat[:, 0:1536], bass.AP(lnx.tensor, 0, [[0, 128], [1, 1536]]), s_lnx, t_gp, t_th)
    TQ = [rows(SL_[0]), rows(SL_[3])]
    t_heads = []
    MEAN, VAR = sm[:, 48:72], sm[:, 72:96]
    for a in range(2):
        ov = OUT[:, a, :].rearrange("p (h d) -> p h d", h=12)
        sqv = TQ[0][:, a, :].rearrange("p (h d) -> p h d", h=12)
        bov = TQ[1][:, a, :].rearrange("p (h d) -> p h d", h=12)
        vv = Vt[:, a, :].rearrange("p (h d) -> p h d", h=12)
        mean, var, bon = MEAN[:, a * 12:(a + 1) * 12], VAR[:, a * 12:(a + 1) * 12], BON[:, a * 12:(a + 1) * 12]

        def wide(t):
            return t.unsqueeze(2).to_broadcast([128, 12, 64])
        g1 = G(lambda e, bov=bov, vv=vv, bon=bon: e.tensor_tensor(bov, vv, wide(bon), ALU.mult), t_bon, t_or)
        t1 = V(lambda e, ov=ov, mean=mean: e.tensor_reduce(mean, ov, AX.X, ALU.add), tq["out"], t_memo)
        t2 = V(lambda e, mean=mean: e.tensor_scalar(mean, mean, 1.0 / 64, None, ALU.mult), t1)
        t3 = V(lambda e, ov=ov, mean=mean: e.tensor_tensor(ov, ov, wide(mean), ALU.subtract), t2)
        t4 = S(lambda e, ov=ov, sqv=sqv: e.activation(sqv, ov, ACT.Square), t3, t_or)
        t5 = V(lambda e, sqv=sqv, var=var: e.tensor_reduce(var, sqv, AX.X, ALU.add), t4)
        t6 = V(lambda e, var=var: e.tensor_scalar(var, var, 1.0 / 64, 64e-5, ALU.mult, ALU.add), t5)
        t7 = S(lambda e, var=var: e.activation(var, var, ACT.Sqrt), t6)
        t8 = V(lambda e, var=var: e.reciprocal(var, var), t7)
        t9 = V(lambda e, ov=ov, var=var: e.tensor_tensor(ov, ov, wide(var), ALU.mult), t8)
        t10 = V(lambda e, a=a: e.tensor_tensor(OUT[:, a, :], OUT[:, a, :], gflat[:, 0:768], ALU.mult), t9, k_lnx)
        t11 = V(lambda e, a=a: e.tensor_tensor(TQ[1][:, a, :], TQ[1][:, a, :], gflat[:, 768:1536], ALU.add), g1, k_lnx)
        t12 = V(lambda e, a=a: e.tensor_tensor(OUT[:, a, :], OUT[:, a, :], TQ[1][:, a, :], ALU.add), t10, t11)
        t_heads.append([V(lambda e, a=a: e.tensor_tensor(OUT[:, a, :], OUT[:, a, :], GK[:, a, :], ALU.mult), t12, t_gk), t_memo])

    def heads_tiles(a, k):
        if k < 6:
            return OUT[:, a, k * 128:(k + 1) * 128]
        return gflat[:, 1536 + a * 256 + (k - 6) * 128:1536 + a * 256 + (k - 5) * 128]

    t_xt, t_tr = turn(heads_tiles, t_heads)
    t_acc = out_proj(t_xt)
    t_x = norm_step(t_acc, 1.0, [6, 7], t_tr)
    arena["free"] = [t_tr]
    t_xt, t_tr = turn(tiles(x), t_x)
    scale_x(t_tr)
    t_acc = ffn(t_xt)
    t_x = norm_step(t_acc, 0.5, [8, 9], t_x)
    t_xt, t_tr = turn(tiles(x), t_x)
    scale_x(t_tr)

    t_acc = ffn(t_xt)
    t_x = norm_step(t_acc, 0.5, [10, 11], t_x)
    t_xt, t_tr = turn(tiles(x), t_x)
    scale_x(t_tr)
    Q, K2, VS = pairs(SL_[0]), pairs(SL_[1]), rows(SL_[2])
    tk = {"q": [], "k": [], "v": []}

    def evac_qk(dst, scale, key):
        def evac(n, b, t):
            o = dst[:, 2 * n:2 * n + 2, :]
            src = P[b][:, :].rearrange("p (s t) -> p s t", s=2)
            if n % 2 == 0:
                k = S(lambda e: e.activation(o, src, ACT.Copy, scale=scale), t, t_acc)
            else:
                k = V(lambda e: e.tensor_scalar(o, src, scale, None, ALU.mult), t, t_acc)
            tk[key].append(k)
            return [k]
        return evac

    T.wait(t_xt)
    proj_cols(3, evac_qk(Q, 0.125, "q"))
    proj_cols(3, evac_qk(K2, 1.0, "k"))
    proj_cols(1, evac_mq)

    def evac_v(o, w):
        def evac(a, b, t):
            k = S(lambda e: e.activation(VS[:, a, o:o + w], P[b][:, 0:w], ACT.Copy), t, t_acc)
            tk["v"].append(k)
            return [k]
        return evac
    proj_rows(512, 2, evac_v(0, 512))
    proj_rows(256, 1, evac_v(512, 256))
    xt["free"] = t_done[st["take"] - 1]
    MN, MB_ = SL_[3][:, 0:384], SL_[3][:, 384:768]
    keep, neg = cs[:, C_KEEP:C_KEEP + 128], cs[:, C_NEG:C_NEG + 128]
    t_m = []
    for o in (0, 256):
        t_m.append(G(lambda e, o=o: e.tensor_scalar(MN[:, o:o + 128], keep, -1.0, None, ALU.mult), t_acc))
        t_m.append(G(lambda e, o=o: e.tensor_copy(MB_[:, o:o + 128], neg), t_acc))
    t_m.append(G(lambda e: e.memset(MN[:, 128:256], -1.0), t_acc))
    t_m.append(G(lambda e: e.memset(MB_[:, 128:256], 0.0), t_acc))
    NA = [SL_[4][:, 384 * i:384 * (i + 1)] for i in range(3)]
    LK = [SL_[5][:, 384 * i:384 * (i + 1)] for i in range(3)]
    EE = [SL_[6][:, 384 * i:384 * (i + 1)] for i in range(3)]
    OB4 = [[0, 1], [2, 3]]
    zb, eb = {}, {}
    tZ, tN, tL, tK, tE2, tA, tX, tP = {}, {}, {}, {}, {}, {}, {}, {}
    OUT = rows(SL_[10])

    def qk(b, h, s, stop_):
        o, j = 64 * (h % 2), h // 2
        d, q0 = ((0, 0), (256, 128))[s]
        mm(P[b][:, d:d + NT - q0], K2[o:o + 64, j, s * 128:(s + 1) * 128], Q[o:o + 64, j, q0:NT], True, stop_)

    def st_a(h):
        b = 4 + h % 2
        T.wait(*pf[b], tk["q"], tk["k"])
        qk(b, h, 0, True)
        qk(b, h, 1, True)
        tZ[h] = T.mark()
        r = h % 3
        tN[h] = S(lambda e: e.activation(NA[r], P[b][:, 0:384], ACT.Abs), tZ[h], tK.get(h - 3))
        t1 = S(lambda e: e.activation(NA[r], NA[r], ACT.Exp, scale=-1.0), tN[h])
        tL[h] = S(lambda e: e.activation(NA[r], NA[r], ACT.Ln, bias=1.0, scale=1.0), t1)

    def st_b(h):
        b, r = 4 + h % 2, h % 3
        t1 = V(lambda e: e.scalar_tensor_tensor(out=LK[r], in0=P[b][:, 0:384], scalar=0.0, in1=NA[r],
                                                op0=ALU.max, op1=ALU.add), tL[h], tE2.get(h - 3))
        pf[b] = [t1]
        tK[h] = V(lambda e: e.tensor_tensor(LK[r], LK[r], MN, ALU.mult), t1, t_m)
        b2 = 6 + h % 2
        T.wait(*pf[b2], tK[h], k_cst)
        tri, ones = cs[:, C_TRI:C_TRI + 128], cs[:, C_ONES:C_ONES + 128]
        qk(b2, h, 0, False)
        mm(P[b2][:, 0:256], tri, LK[r][:, 0:256], False, False)
        mm(P[b2][:, 128:256], ones, LK[r][:, 256:384], False, True)
        qk(b2, h, 1, False)
        mm(P[b2][:, 256:384], tri, LK[r][:, 256:384], False, True)
        tE2[h] = T.mark()

    def st_c(h):
        b2, r = 6 + h % 2, h % 3
        tA[h] = V(lambda e: e.tensor_tensor(EE[r], P[b2][:, 0:384], MB_, ALU.add), tE2[h], tP.get(h - 3), t_m)
        pf[b2] = [tA[h]]
        tX[h] = S(lambda e: e.activation(EE[r], EE[r], ACT.Exp), tA[h])

    def st_d(h):
        r = h % 3
        T.wait(tX[h], tk["v"])
        if h == 0:
            T.wait(pf[0], pf[1], pf[2], pf[3])
        c = (h % 8) * 64
        v = [VS[:, s, h * 64:(h + 1) * 64] for s in range(2)]
        mm(P[OB4[0][h // 8]][:, c:c + 64], EE[r][:, 0:128], v[0])
        mm(P[OB4[1][h // 8]][:, c:c + 64], EE[r][:, 128:256], v[0], True, False)
        mm(P[OB4[1][h // 8]][:, c:c + 64], EE[r][:, 256:384], v[1], False, True)
        tP[h] = T.mark()

    for i in range(12 + 3):
        if i < 12:
            st_a(i)
        if 1 <= i <= 12:
            st_b(i - 1)
        if 2 <= i <= 13:
            st_c(i - 2)
        if 3 <= i:
            st_d(i - 3)
    t_hd2 = []
    for a in range(2):
        k1 = V(lambda e, a=a: e.tensor_copy(OUT[:, a, 0:512], P[OB4[a][0]][:, :]), tP[11], t_acc)
        k2 = S(lambda e, a=a: e.activation(OUT[:, a, 512:768], P[OB4[a][1]][:, 0:256], ACT.Copy), tP[11], t_acc)
        pf[OB4[a][0]], pf[OB4[a][1]] = [k1], [k2]
        t_hd2.append([k1, k2])
    t_memo = mem_attention(MQ, tq["mq"], [gflat[:, 1536:1792], gflat[:, 1792:2048]], AR[:, 11 * 1536:13 * 1536], [t_acc])
    t_heads = [[t_hd2[a], t_memo] for a in range(2)]
    t_xt, t_tr = turn(heads_tiles, t_heads)
    t_acc = out_proj(t_xt)
    t_x = norm_step(t_acc, 1.0, [12, 13], t_tr)
    arena["free"] = [t_tr]
    t_xt, t_tr = turn(tiles(x), t_x)
    scale_x(t_tr)
    t_acc = ffn(t_xt)
    t_x = norm_step(t_acc, 0.5, [14, 15], t_x)
    t_out = dma(Y, out.rearrange("(a p) n -> p a n", p=128), x[:, :, :], s_out, t_x)
    Y.wait(t_out, list(sent.values()))


def build(nc, *aps):
    with ExitStack() as ctx:
        program(nc, ctx, *aps)


def constants():
    p = np.arange(128)
    c = np.zeros((128, C_END + 128), np.float32)
    c[:, C_ID:C_ID + 128] = np.eye(128)
    c[:, C_TRI:C_TRI + 128] = p[:, None] >= p[None, :]
    keep = (p[None, :] > p[:, None]).astype(np.float32)
    c[:, C_KEEP:C_KEEP + 128] = keep
    c[:, C_NEG:C_NEG + 128] = (keep - 1) * BIG
    c[:, C_BLK:C_BLK + 128] = p[:, None] // 64 == p[None, :] // 64
    c[:, C_BLK2:C_BLK2 + 2] = p[:, None] // 64 == np.arange(2)[None, :]
    s, t = (p % 64)[:, None], np.arange(64)[None, :]
    c[:, C_MLT:C_MLT + 64] = s < t
    c[:, C_MLE:C_MLE + 64] = s <= t
    for l in range(6):
        m = 1 << l
        c[:, C_LEV + 64 * l:C_LEV + 64 * l + 64] = (s // (2 * m) == t // (2 * m)) & (s // m % 2 == 0) & (t // m % 2 == 1)
    c[:, C_SCAN:C_SCAN + NT] = np.arange(NT)[None, :] % 64 != 0
    c[:, C_I64:C_I64 + 64] = s == t
    c[:, C_ONES:C_ONES + 128] = 1
    c[:, C_FLIP:C_FLIP + 128] = np.eye(128)[::-1]
    d = 255 - np.arange(512)
    n = np.maximum(d, 1).astype(np.float32)
    large = 16 + (np.log(n / np.float32(16)) / np.float32(math.log(8)) * np.float32(16)).astype(np.int32)
    bucket = np.where(d < 16, np.maximum(d, 0), np.minimum(large, 31))
    base = np.zeros((33, 512), np.float32)
    base[bucket[d >= 0], np.arange(512)[d >= 0]] = 1
    base[32, d < 0] = 1
    return c, base


def by_cols(w, cols):
    return w.reshape(8, 128, -1)[:, :, cols].transpose(1, 0, 2).reshape(128, -1)


def by_rows(w, cols, k0, k1):
    a = w.reshape(8, 128, -1)[k0:k1, :, cols].transpose(1, 0, 2).reshape(128, -1)
    return np.pad(a, ((0, 0), (0, UW - a.shape[1])))


def lay_out(i):
    units = []

    def pair(a, b):
        units.append(np.concatenate([a, b], axis=1))

    def ffn(wg, wu, wd):
        order = [("g", 0), ("g", 1)]
        for j in range(NF // 2):
            if j < NF // 2 - 1:
                order.append(("g", 2 * j + 2))
            order.append(("d", j))
            if j < NF // 2 - 1:
                order.append(("g", 2 * j + 3))
        for kind, n in order:
            if kind == "g":
                cols = slice(128 * n, 128 * n + 128)
                pair(by_cols(wg, cols), by_cols(wu, cols))
            else:
                units.append(wd.reshape(NF // 2, 2, 128, DM)[n].transpose(1, 0, 2).reshape(128, UW))

    def tiles(w, starts):
        c = [by_cols(w, slice(s, s + 128)) for s in starts]
        for n in range(0, len(c), 2):
            pair(c[n], c[n + 1])

    def square(w):
        for n in range(4):
            units.append(w.reshape(4, 2, 128, DM)[n].transpose(1, 0, 2).reshape(128, UW))

    ffn(i["w_ffn1_gate"][0], i["w_ffn1_up"][0], i["w_ffn1_down"][0])
    w = i["w_in"][0]
    t4 = [0, 128, 256, 384]
    tiles(w, t4)
    tiles(w, [512 + t for t in t4])
    for k in (0, 4):
        units.append(by_rows(w, slice(1024, 1536), k, k + 4))
    tiles(w, [1536 + t for t in t4])
    tiles(w, [2048, 2176])
    tiles(w, [2304, 2560])
    cols = list(range(2432, 2560)) + list(range(2688, 2840))
    for k in (0, 4):
        units.append(by_rows(w, cols, k, k + 4))
    for n in ("cmp_w1_k", "cmp_w1_v"):
        c = i[n][0].reshape(2, 8, 128, 256).transpose(0, 2, 1, 3).reshape(2, 128, UW)
        units.extend([c[0], c[1]])
    square(i["w_out"][0])
    ffn(i["w_ffn2_gate"][0], i["w_ffn2_up"][0], i["w_ffn2_down"][0])
    w = i["w_mem_kv_2"]
    tiles(w, [0, 128])
    units.append(by_rows(w, slice(256, 512), 0, 8))
    ffn(i["ffn1_w_gate_2"][0], i["ffn1_w_up_2"][0], i["ffn1_w_down_2"][0])
    tiles(i["rwkv_w_in_2"][0], [128 * t for t in range(22)][:18] + [2304, 2432] + [2560, 2688])
    square(i["w_out_2"][0])
    ffn(i["ffn2_w_gate_2"][0], i["ffn2_w_up_2"][0], i["ffn2_w_down_2"][0])
    ffn(i["ffn1_w_gate_2"][1], i["ffn1_w_up_2"][1], i["ffn1_w_down_2"][1])
    w = i["sb_w_in_2"][0]
    tiles(w, [128 * t for t in range(12)] + [2304, 2432])
    for k in (0, 4):
        units.append(by_rows(w, slice(1536, 2048), k, k + 4))
    units.append(by_rows(w, slice(2048, 2304), 0, 8))
    square(i["w_out_2"][1])
    ffn(i["ffn2_w_gate_2"][1], i["ffn2_w_up_2"][1], i["ffn2_w_down_2"][1])
    assert len(units) == len(unit_kinds())
    ws = np.stack(units)

    def cols_of(v):
        return v.reshape(-1, 128).T

    def positions(v):
        return v[0].reshape(16, 128).T

    vec = np.concatenate([cols_of(i["rwkv_mu_2"][0])] + [cols_of(i[n][0]) for n in (
        "rwkv_w0_2", "rwkv_a0_2", "rwkv_k_k_2", "rwkv_k_a_2")] + [cols_of(i["rwkv_r_k_2"][0].reshape(-1))]
        + [positions(i["cmp_pos_k"]), positions(i["cmp_pos_v"])], axis=1)
    relx = np.concatenate([i["rel_bias"], np.full((1, 16), -BIG, np.float32)])
    g2 = []
    for l in range(2):
        for n in range(3):
            g2 += [i["ln_g_2"][l, n], i["ln_b_2"][l, n]]
    gains = np.stack([i["norm_ffn1"][0], i["norm_mix"][0], i["norm_ffn2"][0], i["norm_final"]] + g2)
    lora = np.concatenate([i["rwkv_w_up_2"][0], i["rwkv_a_up_2"][0]])
    k2, v2 = i["cmp_w2_k"][0].reshape(2, 128, 64), i["cmp_w2_v"][0].reshape(2, 128, 64)
    w2 = np.concatenate([k2[0], k2[0], k2[1], k2[1], v2[0], v2[1]], axis=1)
    cst, base = constants()
    return {
        "ws": ws, "cst": cst, "vec": vec, "base": base, "relx": relx, "gains": gains, "x_in": i["x"][0],
        "mem_in": i["mem_2"][0], "lora": lora, "gup": i["rwkv_g_up_2"][0],
        "lnx": np.stack([i["rwkv_lnx_g_2"][0], i["rwkv_lnx_b_2"][0]]), "w2": w2,
    }


def kernel(**inputs):
    import concourse.bacc as bacc
    from concourse.bass_utils import run_bass_kernel_spmd

    arrays = {k: np.ascontiguousarray(v) for k, v in lay_out({k: np.asarray(v) for k, v in inputs.items()}).items()}
    nc = bacc.Bacc("TRN2", target_bir_lowering=False, num_devices=1)
    aps = [nc.dram_tensor(k, a.shape, mybir.dt.from_np(a.dtype), kind="ExternalInput").ap() for k, a in arrays.items()]
    aps.append(nc.dram_tensor("out", (NT, DM), F32, kind="ExternalOutput").ap())
    build(nc, *aps)
    r = run_bass_kernel_spmd(nc, [arrays], core_ids=[0])
    return r.results[0]["out"].reshape(1, NT, DM)
```

```python
import math
from contextlib import ExitStack

import numpy as np

import concourse.bass as bass
from concourse import mybir

F32 = mybir.dt.float32
F32R = mybir.dt.float32r
ALU = mybir.AluOpType
ACT = mybir.ActivationFunctionType
AX = mybir.AxisListType

NT = 256
DM = 1024
NF = 22
NRAW = 4
NHL = 3
UW = 2048
BIG = 1e30
ALPHA = 4.0 ** 0.25
DECAY = math.exp(-0.5)

C_ID, C_TRI, C_KEEP, C_NEG, C_BLK, C_BLK2 = 0, 128, 256, 384, 512, 640
C_MLT, C_MLE, C_LEV, C_SCAN, C_I64, C_ONES, C_FLIP = 642, 706, 770, 1154, 1410, 1474, 1602
C_END = C_FLIP
C_SEL = C_FLIP + 128
C_ALL = C_SEL + 72 + 768
V_MU, V_W0, V_A0, V_KK, V_KA, V_RK, V_PK, V_PV, V_END = 0, 20, 26, 32, 38, 44, 50, 66, 82


def unit_kinds():
    ffn = [True] * 33
    mixer1 = [True] * 6 + [True, False] * 4 + [True] * 6
    rwkv = [True] * 11 + [True] * 4
    sb = [True] * 10 + [True] * 4
    return ffn + mixer1 + ffn + [True] * 2 + ffn + rwkv + ffn + ffn + sb + ffn


class Queue:

    def __init__(self, engine, sem):
        self.engine, self.sem, self.n, self.seen, self.last = engine, sem, 0, {}, None

    def wait(self, *toks):
        for t in toks:
            if t is None:
                continue
            if isinstance(t, list):
                self.wait(*t)
                continue
            sem, value = t
            if self.seen.get(id(sem), 0) < value:
                self.seen[id(sem)] = value
                self.engine.wait_ge(sem, value)

    def __call__(self, fn, *toks):
        self.wait(*toks)
        self.n += 1
        fn(self.engine).then_inc(self.sem, 1)
        return (self.sem, self.n)

    def quiet(self, fn):
        self.last = fn(self.engine)

    def mark(self):
        self.n += 1
        self.last.then_inc(self.sem, 1)
        return (self.sem, self.n)


def program(nc, ctx, ws, cst, vec, base, relx, gains, x_in, mem_in, lora, gup, lnx, w2, out):
    def sb(name, shape, dt=F32):
        return ctx.enter_context(nc.sbuf_tensor(name, shape, dt))

    def sem(name):
        return ctx.enter_context(nc.semaphore(name))

    raw = [sb(f"raw{i}", [128, UW]) for i in range(NRAW)]
    whi = [sb(f"whi{i}", [128, UW], F32R) for i in range(NHL)]
    wlo = [sb(f"wlo{i}", [128, UW], F32R) for i in range(NHL)]
    x = sb("x", [128, 2, DM])
    xth = sb("xth", [128, 8, NT], F32R)
    xtl = sb("xtl", [128, 8, NT], F32R)
    hh = sb("hh", [128, 3, NT], F32R)
    hl = sb("hl", [128, 3, NT], F32R)
    gb = sb("gb", [128, 2, DM])
    cs = sb("cs", [128, C_END])
    vc = sb("vc", [128, V_END])
    sm = sb("sm", [128, 256])
    AR = sb("AR", [128, 20992])
    P = [ctx.enter_context(nc.psum_tensor(f"P{i}", [128, 512], F32)) for i in range(8)]

    T = Queue(nc.tensor, sem("s_T"))
    V = Queue(nc.vector, sem("s_V"))
    S = Queue(nc.scalar, sem("s_S"))
    G = Queue(nc.gpsimd, sem("s_G"))
    Y = Queue(nc.sync, sem("s_Y"))

    counts, sent = {}, {}

    def dma(q, o, i, s, *toks):
        q.wait(*toks)
        counts[id(s)] = counts.get(id(s), 0) + 16
        q.quiet(lambda e: e.dma_start(o, i).then_inc(s, 16))
        sent[id(s)] = (s, counts[id(s)])
        return sent[id(s)]

    s_raw = [sem(f"s_raw{i}") for i in range(NRAW)]
    s_cst, s_vec, s_x0, s_x1, s_gn, s_base, s_rel, s_mem = (sem(f"s_{n}") for n in (
        "cst", "vec", "x0", "x1", "gn", "base", "rel", "mem"))
    s_flip, s_sel, s_id = sem("s_flip"), sem("s_sel"), sem("s_id")
    s_dist = [sem(f"s_dist{i}") for i in range(2)]
    s_dup = [sem(f"s_dup{i}") for i in range(8)]
    s_lora, s_gup, s_lnx, s_w2, s_out = (sem(f"s_{n}") for n in ("lora", "gup", "lnx", "w2", "out"))

    ident = cs[:, C_ID:C_ID + 128]

    kinds = unit_kinds()
    nu = len(kinds)
    sidx = np.cumsum([0] + kinds)[:-1]
    t_load, t_hi, t_lo, t_done = {}, {}, {}, {}
    st = {"dma": 0, "hi": 0, "split": 0, "take": 0}
    split_units = [u for u in range(nu) if kinds[u]]

    def pump():
        while st["dma"] < nu:
            u = st["dma"]
            old = u - NRAW
            if old >= 0:
                need = t_lo.get(old) if kinds[old] else t_done.get(old)
                if need is None:
                    return
            else:
                need = None
            t_load[u] = dma(Y, raw[u % NRAW][:, :], ws[u, :, :], s_raw[u % NRAW], need)
            st["dma"] += 1

    def split_hi(v):
        while st["hi"] <= v and st["hi"] < nu:
            u = st["hi"]
            st["hi"] += 1
            if not kinds[u]:
                continue
            i = int(sidx[u])
            slot = i % NHL
            free = t_done[split_units[i - NHL]] if i >= NHL else None
            pump()
            r, h = raw[u % NRAW], whi[slot]
            t_hi[u] = S(lambda e: e.activation(h[:, :], r[:, :], ACT.Copy), t_load[u], free)

    def split(v):
        while st["split"] <= v and st["split"] < nu:
            u = st["split"]
            st["split"] += 1
            split_hi(u)
            if not kinds[u]:
                continue
            i = int(sidx[u])
            slot = i % NHL
            free = t_done[split_units[i - NHL]] if i >= NHL else None
            r, h, l = raw[u % NRAW], whi[slot], wlo[slot]
            t_lo[u] = V(lambda e: e.tensor_tensor(l[:, :], r[:, :], h[:, :].bitcast(F32), ALU.subtract),
                        t_hi[u], t_load[u], free)
            pump()

    def reach(ahead):
        v = st["take"]
        for j in range(v + 1, min(v + ahead + 1, nu)):
            if kinds[j]:
                i = int(sidx[j])
                if i >= NHL and split_units[i - NHL] not in t_done:
                    break
            v = j
        return v

    def take(ahead=2):
        u = st["take"]
        split(u)
        split(reach(ahead))
        st["take"] += 1
        pump()
        if not kinds[u]:
            return u, raw[u % NRAW], None, t_load[u]
        slot = int(sidx[u]) % NHL
        return u, whi[slot], wlo[slot], t_lo[u]

    def done(u, tok):
        t_done[u] = tok
        pump()

    pf = [[] for _ in range(8)]
    ring = {"i": 0, "over": list(range(8))}

    def bank():
        ring["i"] += 1
        b = ring["over"][ring["i"] % len(ring["over"])]
        T.wait(*pf[b])
        pf[b] = []
        return b

    def mm(o, l, r, start=True, stop=True):
        T.quiet(lambda e: e.matmul(o, l, r, start=start, stop=stop, skip_group_check=True))

    def mm3(o, ah, al, bh, bl, start, stop):
        mm(o, ah, bh, start, False)
        mm(o, ah, bl, False, False)
        mm(o, al, bh, False, stop)

    def tr(o, i, n=128, base=0):
        T.quiet(lambda e: e.transpose(o, i, cs[base:base + n, C_ID + base:C_ID + base + n]))

    def warm(n):
        for _ in range(n):
            mm(P[7][:, :], xth[:, 0, 0:128], xth[:, 0:2, :])

    k_x = [dma(q, x[:, i, :], x_in[i * 128:(i + 1) * 128, :], s) for i, s, q in ((0, s_x0, Y), (1, s_x1, S))]

    def load_gains(rows, *toks, q=Y):
        t = None
        for j, r in enumerate(rows):
            src = bass.AP(gains.tensor, r * DM, [[0, 128], [1, DM]])
            if j == 0:
                t = dma(q, gb[:, 0, :], src, s_gn, *toks)
            else:
                t = dma(q, gb[:, 1, :], src, s_gn2, *toks)
        return [(s_gn, counts[id(s_gn)])] + ([(s_gn2, counts[id(s_gn2)])] if len(rows) > 1 else [])

    s_gn2 = sem("s_gn2")
    t_g = load_gains([0], q=S)
    k_id = dma(G, cs[:, 0:C_TRI], cst[:, 0:C_TRI], s_id)
    Y.wait(k_x, t_g)
    pump()
    k_vec = dma(Y, vc[:, :], vec[:, :], s_vec)
    k_cst = dma(Y, cs[:, C_TRI:C_END], cst[:, C_TRI:C_END], s_cst)

    XN = AR[:, 0:2048].rearrange("p (a n) -> p a n", a=2)
    SL = AR[:, 2048:2560].rearrange("p (a n) -> p a n", a=2)
    HF = AR[:, 2560:3072].rearrange("p (a n) -> p a n", a=2)

    def rms(t_x, t_gain, xn_free):
        toks = []
        for a in range(2):
            t1 = S(lambda e: e.activation(XN[:, a, :], x[:, a, :], ACT.Square, accum_out=sm[:, 4 + a:5 + a]), t_x[a], xn_free)
            t2 = V(lambda e: e.tensor_scalar(sm[:, 10 + a:11 + a], sm[:, 4 + a:5 + a], 1.0 / DM, 1e-6, ALU.mult, ALU.add), t1)
            t3 = S(lambda e: e.activation(sm[:, 6 + a:7 + a], sm[:, 10 + a:11 + a], ACT.Sqrt), t2)
            t4 = V(lambda e: e.reciprocal(sm[:, 10 + a:11 + a], sm[:, 6 + a:7 + a]), t3)
            q = []
            for h in range(2):
                c = slice(512 * h, 512 * h + 512)
                q.append(V(lambda e: e.scalar_tensor_tensor(out=XN[:, a, c], in0=x[:, a, c], scalar=sm[:, 10 + a:11 + a],
                                                            in1=gb[:, 0, c], op0=ALU.mult, op1=ALU.mult), t4, t_gain, t1))
            toks.append(q)
        return toks

    def norm_step(t_acc, scale, t_gain):
        t0, tm, t1, t3, toks = {}, {}, {}, {}, []
        for a in range(2):
            t0[a] = []
            for h in range(2):
                xs = x[:, a, 512 * h:512 * h + 512]
                b = 2 * a + h
                t0[a].append(V(lambda e: e.tensor_tensor_reduce(xs, P[b][:, :], xs, 1.0, 0.0, ALU.add, ALU.add,
                                                                sm[:, b:b + 1]), t_acc[a], t_alpha["v"]))
                pf[b] = [t0[a][-1]]
            tm[a] = V(lambda e: e.tensor_scalar(sm[:, 8 + a:9 + a], sm[:, 2 * a:2 * a + 1], sm[:, 2 * a + 1:2 * a + 2],
                                                -1.0 / DM, ALU.add, ALU.mult), t0[a])
            junk = xtl[:, 4 * a:4 * a + 4, :].rearrange("p k n -> p (k n)")
            t1[a] = S(lambda e: e.activation(junk, x[:, a, :], ACT.Square, bias=sm[:, 8 + a:9 + a],
                                             accum_out=sm[:, 4 + a:5 + a]), tm[a], t0[a], xt["free"])
        for a in range(2):
            t2 = V(lambda e: e.tensor_scalar(sm[:, 10 + a:11 + a], sm[:, 4 + a:5 + a], 1.0 / DM, 1e-5 / scale ** 2,
                                             ALU.mult, ALU.add), t1[a])
            t3 = S(lambda e: e.activation(sm[:, 6 + a:7 + a], sm[:, 10 + a:11 + a], ACT.Sqrt), t2)
            q = []
            for h in range(2):
                c = slice(512 * h, 512 * h + 512)
                q.append(V(lambda e: e.scalar_tensor_tensor(out=x[:, a, c], in0=x[:, a, c], scalar=sm[:, 8 + a:9 + a],
                                                            in1=gb[:, 0, c], op0=ALU.add, op1=ALU.mult), t1[a], t_gain))
            t4 = V(lambda e: e.reciprocal(sm[:, 10 + a:11 + a], sm[:, 6 + a:7 + a]), t3)
            r = []
            for h in range(2):
                c = slice(512 * h, 512 * h + 512)
                r.append(V(lambda e: e.scalar_tensor_tensor(out=x[:, a, c], in0=x[:, a, c], scalar=sm[:, 10 + a:11 + a],
                                                            in1=gb[:, 1, c], op0=ALU.mult, op1=ALU.add), t4, q))
            toks.append(r)
        return toks

    def root_next():
        S(lambda e: e.activation(sm[:, 31:32], cs[:, C_ONES:C_ONES + 1], ACT.Sqrt), k_cst)

    xt = {"free": None}

    def turn(src, toks, banks=(4, 5, 6, 7), ks=range(8), by_quarter=True):
        ready, banks, n, last = [[], []], list(banks), 0, []
        ks = list(ks)
        for a in range(2):
            for g in range(0, len(ks), 4):
                kk = ks[g:g + 4]
                need = toks[a][g // 4] if by_quarter else toks[a]
                b = banks[n % len(banks)]
                n += 1
                T.wait(*pf[b], need, k_id)
                for j, k in enumerate(kk):
                    tr(P[b][:, j * 128:(j + 1) * 128], src(a, k))
                t0 = T.mark()
                last.append(t0)
                w = len(kk) * 128
                pv = P[b][:, 0:w].rearrange("p (k n) -> p k n", k=len(kk))
                oh = xth[:, kk[0]:kk[0] + len(kk), a * 128:(a + 1) * 128]
                ol = xtl[:, kk[0]:kk[0] + len(kk), a * 128:(a + 1) * 128]
                t1 = S(lambda e, pv=pv, oh=oh: e.activation(oh, pv, ACT.Copy), t0, xt["free"])
                t2 = V(lambda e, pv=pv, oh=oh, ol=ol: e.tensor_tensor(ol, pv, oh.bitcast(F32), ALU.subtract), t1, xt["free"])
                pf[b] = [t1, t2]
                ready[g // 4] += [t1, t2]
        return ready, last

    def tiles(t):
        return lambda a, k: t[:, a, k * 128:(k + 1) * 128]

    arena = {"free": []}

    def ffn(t_xt, filler=None):
        lo, sl_free, hf_free, hh_free = {}, {}, {}, {}
        first = {"v": True}

        def gate_up(f):
            u, wh, wl, tw = take()
            b = 4 + f % 3
            T.wait(tw, t_xt[0], *pf[b])
            for s in range(2):
                for k in range(8):
                    if k == 4:
                        T.wait(t_xt[1])
                    c = (s * 8 + k) * 128
                    mm3(P[b][:, s * NT:(s + 1) * NT], wh[:, c:c + 128], wl[:, c:c + 128],
                        xth[:, k, :], xtl[:, k, :], k == 0, k == 7)
            t = T.mark()
            done(u, t)
            i, j = f % 2, f % 3
            t1 = S(lambda e: e.activation(SL[:, i, :], P[b][:, 0:NT], ACT.Silu), t, sl_free.get(f - 2), arena["free"])
            t2 = V(lambda e: e.tensor_tensor(HF[:, i, :], P[b][:, NT:2 * NT], SL[:, i, :], ALU.mult), t1, hf_free.get(f - 2))
            sl_free[f] = t2
            pf[b] = [t1, t2]
            t3 = S(lambda e: e.activation(hh[:, j, :], HF[:, i, :], ACT.Copy), t2, hh_free.get(f - 3))
            t4 = V(lambda e: e.tensor_tensor(hl[:, j, :], HF[:, i, :], hh[:, j, :].bitcast(F32), ALU.subtract), t3)
            hf_free[f] = [t3, t4]
            lo[f] = t4
            return t

        def down(j):
            u, wh, wl, tw = take(2 if j < NF // 2 - 1 else 1)
            T.wait(tw)
            last = j == NF // 2 - 1
            ta = []
            for i, a in ((0, 0), (1, 0), (0, 1), (1, 1)) if last else ((0, 0), (0, 1), (1, 0), (1, 1)):
                f = 2 * j + i
                T.wait(lo[f])
                for h in range(2):
                    if f == 0:
                        T.wait(*pf[2 * a + h])
                    c = i * DM + h * 512
                    mm3(P[2 * a + h][:, :], hh[:, f % 3, a * 128:(a + 1) * 128], hl[:, f % 3, a * 128:(a + 1) * 128],
                        wh[:, c:c + 512], wl[:, c:c + 512], f == 0, f == NF - 1)
                ta.append(T.mark())
                hh_free[f] = ta[-1]
            done(u, ta[-1])
            return [ta[1], ta[3]]

        gate_up(0)
        gate_up(1)
        for j in range(NF // 2):
            if j < NF // 2 - 1:
                gate_up(2 * j + 2)
            t = down(j)
            if j < NF // 2 - 1:
                tl = gate_up(2 * j + 3)
                if 2 * j + 3 == NF - 1:
                    xt["free"] = tl
                    root_next()
            if filler is not None:
                filler(j)
        arena["free"] = []
        return t

    def residual(t_acc, scale):
        toks = []
        for a in range(2):
            r = []
            for h in range(2):
                xs = x[:, a, h * 512:(h + 1) * 512]
                t = V(lambda e, xs=xs, b=2 * a + h: e.scalar_tensor_tensor(out=xs, in0=P[b][:, :], scalar=scale, in1=xs,
                                                                          op0=ALU.mult, op1=ALU.add), t_acc[a], t_alpha["v"])
                pf[2 * a + h] = [t]
                r.append(t)
            toks.append(r)
        return toks

    t_alpha = {"v": None}

    def scale_x(scale, *toks):
        t_alpha["v"] = [G(lambda e, a=a: e.tensor_scalar(x[:, a, :], x[:, a, :], ALPHA / scale, None, ALU.mult), *toks)
                        for a in range(2)]

    def proj_cols(n_units, evac):
        for n in range(n_units):
            u, wh, wl, tw = take()
            b = bank()
            T.wait(tw)
            for s in range(2):
                for k in range(8):
                    c = (s * 8 + k) * 128
                    mm3(P[b][:, s * NT:(s + 1) * NT], wh[:, c:c + 128], wl[:, c:c + 128],
                        xth[:, k, :], xtl[:, k, :], k == 0, k == 7)
            t = T.mark()
            done(u, t)
            pf[b] = evac(n, b, t)
            if st["take"] < nu:
                split_hi(reach(2))

    def proj_rows(width, n_units, evac, between=None):
        bb = [bank(), bank()]
        per = 8 // n_units
        for n in range(n_units):
            u, wh, wl, tw = take()
            T.wait(tw)
            for k in range(per):
                kk = n * per + k
                for a in range(2):
                    mm3(P[bb[a]][:, 0:width], xth[:, kk, a * 128:(a + 1) * 128], xtl[:, kk, a * 128:(a + 1) * 128],
                        wh[:, k * width:(k + 1) * width], wl[:, k * width:(k + 1) * width], kk == 0, kk == 7)
            t = T.mark()
            done(u, t)
            if between is not None and n < n_units - 1:
                split_hi(reach(2))
                between()
        for a in range(2):
            pf[bb[a]] = evac(a, bb[a], t)

    def out_steps(t_xt, order, res):
        for n in order:
            last = n == order[-1]
            u, wh, wl, tw = take(1 if last else 2)
            T.wait(tw)
            for i, a in ((0, 0), (1, 0), (0, 1), (1, 1)):
                k = 2 * n + i
                T.wait(t_xt[k // 4])
                for h in range(2):
                    if (n, i) == (order[0], 0):
                        T.wait(*pf[2 * a + h])
                    c = i * DM + h * 512
                    mm3(P[2 * a + h][:, :], xth[:, k, a * 128:(a + 1) * 128], xtl[:, k, a * 128:(a + 1) * 128],
                        wh[:, c:c + 512], wl[:, c:c + 512], (n, i) == (order[0], 0), last and i == 1)
                if (i, a) == (1, 0):
                    ta = T.mark()
                    if not last:
                        yield
            t = T.mark()
            done(u, t)
            if last:
                xt["free"] = t
                res += [ta, t]
            yield

    def out_proj(t_xt):
        res = []
        for _ in out_steps(t_xt, (0, 1, 2, 3), res):
            pass
        return res

    def attend(units, L, Pr, Pt, mx, den, OB, res, rs, rp):
        n = len(units)
        tS, tE, tT, tC, tPV = {}, {}, {}, {}, {}
        sb_, pb_ = {}, {}
        nL = len(L)

        def wd(u):
            return [(0, 128), (128, 256)] if u["bias"] is not None else [(0, 256), (256, 256)]

        def s0(i):
            u = units[i]
            b = rs[i % len(rs)]
            T.wait(*pf[b], u["need"])
            for a in range(2):
                o, w = wd(u)[a]
                mm(P[b][:, o:o + w], u["q"][:, a * 128:(a + 1) * 128], u["k"][:, 0:w])
            tS[i] = T.mark()
            sb_[i] = b

        def s1(i):
            u, b, r = units[i], sb_[i], i % nL
            ex, tm = [], []
            for a in range(2):
                o, w = wd(u)[a]
                m = mx[:, 4 * (i % 4) + a:4 * (i % 4) + a + 1]
                if u["bias"] is not None:
                    bi = u["bias"][:, 128:256] if a == 0 else u["bias"]
                    tm.append(V(lambda e, o=o, w=w, m=m, bi=bi: e.tensor_tensor_reduce(
                        L[r][:, o:o + w], P[b][:, o:o + w], bi, 1.0, -3e38, ALU.add, ALU.max, m), tS[i], tE.get(i - nL)))
                else:
                    tm.append(V(lambda e, o=o, w=w, m=m: e.tensor_reduce(m, P[b][:, o:o + w], AX.X, ALU.max), tS[i],
                                tE.get(i - 4)))
            nm = mx[:, 4 * (i % 4) + 2:4 * (i % 4) + 4]
            t = V(lambda e: e.tensor_scalar(nm, mx[:, 4 * (i % 4):4 * (i % 4) + 2], -1.0, None, ALU.mult), *tm)
            for a in range(2):
                o, w = wd(u)[a]
                src = L[r] if u["bias"] is not None else P[b]
                ex.append(S(lambda e, a=a, o=o, w=w, src=src: e.activation(
                    Pr[r][:, o:o + w], src[:, o:o + w], ACT.Exp, bias=nm[:, a:a + 1], scale=1.0,
                    accum_out=den[:, 2 * u["slot"] + a:2 * u["slot"] + a + 1]), t, tT.get(i - nL), *u.get("hold", [])))
            tE[i] = ex
            pf[b] = tm if u["bias"] is not None else ex

        def s2(i):
            u, r = units[i], i % nL
            b = rp[i % len(rp)]
            T.wait(*pf[b], tE[i])
            blocks = [0, 128, 256] if u["bias"] is not None else [0, 128, 256, 384]
            for j in blocks:
                tr(P[b][:, j:j + 128], Pr[r][:, j:j + 128])
            tT[i] = T.mark()
            w = blocks[-1] + 128
            q = V if i % 3 else S
            if q is V:
                tC[i] = V(lambda e: e.tensor_copy(Pt[r][:, 0:w], P[b][:, 0:w]), tT[i], tPV.get(i - nL))
            else:
                tC[i] = S(lambda e: e.activation(Pt[r][:, 0:w], P[b][:, 0:w], ACT.Copy), tT[i], tPV.get(i - nL))
            pf[b] = [tC[i]]

        def s3(i):
            u, r = units[i], i % nL
            T.wait(tC[i], u["needv"])
            c = u["col"]
            if i == 0:
                T.wait(*pf[OB[0]], *pf[OB[1]])
            if u["bias"] is not None:
                parts = [(0, [(0, 0)]), (1, [(128, 0), (256, 1)])]
            else:
                parts = [(0, [(0, 0), (128, 1)]), (1, [(256, 0), (384, 1)])]
            for a, lst in parts:
                for j, (o, s) in enumerate(lst):
                    mm(P[OB[a]][:, c:c + 64], Pt[r][:, o:o + 128], u["v"](s), j == 0, j == len(lst) - 1)
            tPV[i] = T.mark()

        for i in range(n + 2):
            if i < n:
                s0(i)
                s1(i)
            if 1 <= i <= n:
                s2(i - 1)
            if 2 <= i:
                s3(i - 2)
            if i == n + 1:
                res += [tPV[n - 1], [tE[i] for i in range(n)]]
            yield

    def run(steps, n=None):
        if n is None:
            for _ in steps:
                pass
        else:
            for _ in range(n):
                next(steps, None)

    BIAS = AR[:, 3072:7168].rearrange("p (h c) -> p h c", h=16)
    CB = AR[:, 20352:20592].rearrange("p (h a n) -> p h a n", h=8, a=2)
    HANK = AR[:, 7168:13312].rearrange("p (h c) -> p h c", h=16)
    BASE = AR[0:33, 13312:13824]
    RELX = AR[0:33, 13824:13840]
    VALS = AR[0:16, 13840:14352]
    FLIP = AR[:, 14352:14480]
    k_flip = dma(G, FLIP, cst[:, C_FLIP:C_FLIP + 128], s_flip)
    k_base = dma(G, BASE, base[:, :], s_base)
    k_rel = dma(G, RELX, relx[:, :], s_rel)

    t_xn = rms([[k_x[0]] * 2, [k_x[1]] * 2], t_g, None)
    t_xt, t_tr = turn(tiles(XN), t_xn)

    hank = {}

    def by_distance():
        T.wait(k_base, k_rel, *pf[7])
        mm(P[7][0:16, :], RELX, BASE)
        t = T.mark()
        t1 = V(lambda e: e.tensor_copy(VALS, P[7][0:16, :]), t)
        pf[7] = [t1]
        dist = nc.dram_tensor("by_distance", (16, 512), F32).ap()
        t2 = dma(G, dist[:, :], VALS, s_dist[0], t1)
        hank["k"] = dma(G, HANK, bass.AP(dist.tensor, 0, [[1, 128], [512, 16], [1, 384]]), s_dist[1], t2)

    t_bias = []

    def bias_part(r):
        T.wait(hank["k"], k_flip, *pf[7])
        if r < 8:
            mm(P[7][:, :], FLIP, HANK[:, 2 * r:2 * r + 2, 0:256])
            t = T.mark()
            t1 = S(lambda e: e.activation(BIAS[:, 2 * r:2 * r + 2, :], P[7][:, :].rearrange("p (h c) -> p h c", h=2),
                                          ACT.Copy), t)
        else:
            for a in range(2):
                c = 159 - 128 * a
                mm(P[7][:, a * 120:(a + 1) * 120], FLIP, HANK[:, 8:16, c:c + 225:16])
            t = T.mark()
            t1 = S(lambda e: e.activation(CB, P[7][:, 0:240].rearrange("p (a h n) -> p h a n", a=2, h=8), ACT.Copy), t)
        pf[7] = [t1]
        t_bias.append(t1)

    t_g = load_gains([1], t_xn)
    def biases(j):
        if j == 0:
            by_distance()
        if j > 2:
            bias_part(j - 3)
        if j == 10:
            bias_part(8)

    t_acc = ffn(t_xt, biases)
    t_x = residual(t_acc, 0.5)
    t_xn = rms(t_x, t_g, t_tr)
    t_xt, t_tr = turn(tiles(XN), t_xn)

    def ar(a, n, s=None):
        v = AR[:, a:a + n]
        return v if s is None else v.rearrange(*s[0], **s[1])

    QA = ar(7168, 1024, (("p (j t) -> p j t",), dict(j=4)))
    KA = ar(8192, 1024, (("p (j t) -> p j t",), dict(j=4)))
    QB = ar(9216, 1024, (("p (j t) -> p j t",), dict(j=4)))
    KS2 = ar(10240, 512, (("p (g t) -> p g t",), dict(g=2)))
    KW2 = ar(10752, 512, (("p (g t) -> p g t",), dict(g=2)))
    VA = ar(11264, 1024, (("p (a c) -> p a c",), dict(a=2)))
    VG = ar(12288, 560, (("p (a c) -> p a c",), dict(a=2)))
    KV = ar(12848, 512, (("p (s t) -> p s t",), dict(s=2)))
    KSW = ar(13360, 512, (("p (s t) -> p s t",), dict(s=2)))
    X2 = ar(13872, 1024, (("p (s g t) -> p s g t",), dict(s=2, g=2)))
    BK = ar(14896, 960, (("p (s l g n) -> p s l g n",), dict(s=2, l=16, g=2)))
    LR = [ar(15856 + 384 * i, 384) for i in range(3)]
    PR = [ar(17008 + 384 * i, 384) for i in range(3)]
    PT = [ar(18160 + 384 * i, 384) for i in range(3)]
    HD = ar(19312, 120, (("p (s m n) -> p s m n",), dict(s=2, m=2)))
    KC2 = ar(19432, 30)
    VC = ar(19464, 128, (("p (g d) -> p g d",), dict(g=2)))
    W2 = ar(19592, 384)
    O = ar(0, 2048, (("p (a n) -> p a n",), dict(a=2)))
    CL = ar(2048, 240, (("p (h a n) -> p h a n",), dict(h=8, a=2)))
    CP = ar(2304, 240, (("p (h a n) -> p h a n",), dict(h=8, a=2)))
    CT = ar(13800, 2048)
    MX = sm[:, 32:48]
    DEN = sm[:, 48:112]
    GT = sm[:, 112:160]
    CMX = sm[:, 160:176]
    CDEN = sm[:, 176:192]
    RD = sm[:, 192:256]

    k_w2 = dma(G, W2, w2[:, :], s_w2)
    tq = {}

    def copy_to(dst, scale, key, w=2):
        def evac(n, b, t):
            o = dst[:, 2 * n:2 * n + 2, :]
            src = P[b][:, :].rearrange("p (s t) -> p s t", s=2)
            if n % 2 == 0:
                k = S(lambda e: e.activation(o, src, ACT.Copy, scale=scale), t)
            else:
                k = V(lambda e: e.tensor_scalar(o, src, scale, None, ALU.mult), t)
            tq.setdefault(key, []).append(k)
            return [k]
        return evac

    def evac_va(a, b, t):
        k = S(lambda e: e.activation(VA[:, a, :], P[b][:, :], ACT.Copy), t)
        tq.setdefault("va", []).append(k)
        return [k]

    def evac_vg(a, b, t):
        k = V(lambda e: e.tensor_copy(VG[:, a, 0:256], P[b][:, 0:256]), t)
        k2 = S(lambda e: e.activation(GT[:, a * 24:(a + 1) * 24], P[b][:, 256:280], ACT.Sigmoid), k)
        tq.setdefault("vg", []).extend([k, k2])
        return [k, k2]

    T.wait(t_xt)
    ring["over"] = [0, 1]
    proj_cols(1, copy_to(KV, 1.0, "kv"))
    proj_cols(1, copy_to(KSW, 1.0, "ksw"))

    dups = []
    for i, (dst, s) in enumerate(((KS2, 0), (KW2, 1))):
        t1 = dma(G, dst[64:128, 0, :], KSW[0:64, s, :], s_dup[2 * i], tq["ksw"])
        t2 = dma(G, dst[0:64, 1, :], KSW[64:128, s, :], s_dup[2 * i + 1], tq["ksw"])
        t3 = G(lambda e, dst=dst, s=s: e.tensor_copy(dst[0:64, 0, :], KSW[0:64, s, :]), tq["ksw"])
        t4 = G(lambda e, dst=dst, s=s: e.tensor_copy(dst[64:128, 1, :], KSW[64:128, s, :]), tq["ksw"])
        dups.append([t1, t2, t3, t4])
    xk = []
    for s in range(2):
        t1 = dma(G, X2[64:128, s, 0, 0:255], KV[0:64, s, 1:256], s_dup[4 + 2 * s], tq["kv"])
        t2 = dma(G, X2[0:64, s, 1, :], KV[64:128, s, :], s_dup[5 + 2 * s], tq["kv"])
        t3 = G(lambda e, s=s: e.tensor_copy(X2[0:64, s, 0, :], KV[0:64, s, :]), tq["kv"])
        t4 = G(lambda e, s=s: e.tensor_copy(X2[64:128, s, 1, 0:255], KV[64:128, s, 1:256]), tq["kv"])
        xk.append([t1, t2, t3, t4])

    proj_rows(280, 2, evac_vg)
    proj_cols(2, copy_to(QB, 0.125, "qb"))
    t_bk = []
    for s in range(2):
        for g in range(2):
            base_ap = X2[:, s, g, :]
            src = bass.AP(base_ap.tensor, base_ap.offset, [list(base_ap.ap[0]), [2, 16], [16, 15]])
            pos = vc[:, V_PK + 16 * s:V_PK + 16 * s + 16].unsqueeze(2).to_broadcast([128, 16, 15])
            t_bk.append(V(lambda e, s=s, g=g, src=src, pos=pos: e.tensor_tensor(BK[:, s, :, g, :], src, pos, ALU.add),
                          xk[s], k_vec))
    HT = ar(2560, 512, (("p (s n) -> p s n",), dict(s=2)))
    TM = ar(2560, 512)
    t_hd, t_htp = [], []

    def compress(s, half):
        b = 4 + s
        u, w, _, tw = take()
        T.wait(tw, t_bk)
        if half == 0:
            T.wait(*pf[b])
        for l in range(8):
            lp = half * 8 + l
            mm(P[b][0:30, 0:256], BK[:, s, lp, :, :].rearrange("p g n -> p (g n)"), w[:, l * 256:(l + 1) * 256],
               lp == 0, lp == 15)
        t = T.mark()
        done(u, t)
        if half == 1:
            pf[b] = [S(lambda e: e.activation(HT[0:30, s, :], P[b][0:30, 0:256], ACT.Silu), t, t_tr)]

    def compressed(s):
        b = 4 + s
        T.wait(*pf[b])
        for m in range(2):
            T.quiet(lambda e: e.transpose(P[b][:, 30 * m:30 * m + 30], HT[0:30, s, 128 * m:128 * m + 128],
                                          cs[0:30, C_ID:C_ID + 30]))
        t = T.mark()
        t_htp.append(t)
        k = V(lambda e: e.tensor_copy(HD[:, s, :, :], P[b][:, 0:60].rearrange("p (m n) -> p m n", m=2)), t)
        pf[b] = [k]
        t_hd.append(k)

    t_kc, t_ct, t_o = [], [], []

    def compressed_attention():
        ring["over"], over = [6, 7], ring["over"]
        b = bank()
        T.wait(t_hd, k_w2)
        for m in range(2):
            mm(P[b][:, 0:30], W2[:, m * 128:(m + 1) * 128], HD[:, 0, m, :], m == 0, m == 1)
        for g in range(2):
            for m in range(2):
                mm(P[b][0:15, 64 + 64 * g:128 + 64 * g], HD[:, 1, m, g * 15:(g + 1) * 15],
                   W2[:, 256 + m * 64:256 + (m + 1) * 64], m == 0, m == 1)
        t = T.mark()
        t1 = V(lambda e: e.tensor_copy(KC2, P[b][:, 0:30]), t)
        t2 = V(lambda e: e.tensor_copy(VC[0:15, :, :], P[b][0:15, 64:192].rearrange("p (g d) -> p g d", g=2)), t)
        pf[b] = [t1, t2]
        t_kc.extend([t1, t2])
        ring["over"] = over
        yield
        ring["over"] = [6, 7]
        b2 = [bank(), bank()]
        T.wait(t_kc, tq["qb"])
        for h in range(8):
            o = 64 * (h % 2)
            for a in range(2):
                c = (h // 2 * 2 + a) * 15
                mm(P[b2[h % 2]][:, c:c + 15], QB[o:o + 64, h // 2, a * 128:(a + 1) * 128],
                   KC2[o:o + 64, 15 * (h // 4):15 * (h // 4) + 15])
        t = T.mark()
        t1 = []
        for i in range(2):
            t1.append(V(lambda e: e.tensor_tensor(CL[:, i:8:2, :, :],
                                                  P[b2[i]][:, 0:120].rearrange("p (h a n) -> p h a n", h=4, a=2),
                                                  CB[:, i:8:2, :, :], ALU.add), t, t_bias, t_tr))
            pf[b2[i]] = [t1[-1]]
        ring["over"] = over
        CLv = CL.rearrange("p h a n -> p (h a) n")
        CPv = CP.rearrange("p h a n -> p (h a) n")
        t2 = V(lambda e: e.tensor_reduce(CMX, CLv, AX.X, ALU.max), t1)
        t3 = V(lambda e: e.tensor_scalar(CMX, CMX, -1e20, None, ALU.max), t2)
        t4 = V(lambda e: e.tensor_tensor(CLv, CLv, CMX.unsqueeze(2).to_broadcast([128, 16, 15]), ALU.subtract), t3)
        yield
        t5 = S(lambda e: e.activation(CPv, CLv, ACT.Exp), t4)
        t6 = V(lambda e: e.tensor_reduce(CDEN, CPv, AX.X, ALU.add), t5)
        t7 = V(lambda e: e.tensor_scalar(CDEN, CDEN, 1e-30, None, ALU.max), t6)
        t8 = V(lambda e: e.reciprocal(CDEN, CDEN), t7)
        t9 = V(lambda e: e.tensor_tensor(CDEN.rearrange("p (h a) -> p a h", a=2), CDEN.rearrange("p (h a) -> p a h", a=2),
                                         GTv[:, :, :, 0], ALU.mult), t8, tq["vg"])
        yield
        for q4 in range(4):
            ring["over"] = [6, 7]
            b = bank()
            ring["over"] = over
            T.wait(t5)
            for j in range(4):
                i = 4 * q4 + j
                tr(P[b][0:15, j * 128:(j + 1) * 128], CPv[:, i, :])
            t = T.mark()
            t_ct.append(S(lambda e, b=b, q4=q4: e.activation(CT[0:15, q4 * 512:(q4 + 1) * 512], P[b][0:15, :], ACT.Copy), t,
                          t_w1, dups))
            pf[b] = [t_ct[-1]]
            if q4 % 2:
                yield
        ring["over"] = [6, 7]
        ob = [bank(), bank()]
        ring["over"] = over
        T.wait(t_ct, t_kc)
        for h in range(8):
            for a in range(2):
                i = 2 * h + a
                mm(P[ob[a]][:, h * 64:(h + 1) * 64], CT[0:15, i * 128:(i + 1) * 128], VC[0:15, h // 4, :])
        t = T.mark()
        for a in range(2):
            cf = CDEN.rearrange("p (h a) -> p a h", a=2)[:, a, :].unsqueeze(2).to_broadcast([128, 8, 64])
            k = V(lambda e: e.tensor_tensor(TM.rearrange("p (h d) -> p h d", h=8),
                                            P[ob[a]][:, :].rearrange("p (h d) -> p h d", h=8), cf, ALU.mult),
                  t, t9, t_nsa[0], t_nsa[1])
            pf[ob[a]] = [k]
            t_nsa[a] = V(lambda e: e.tensor_tensor(O[:, a, 512:1024], O[:, a, 512:1024], TM, ALU.add), k)
        yield

    def heads(which):
        us = []
        for h in range(8):
            o, j, g = 64 * (h % 2), h // 2, h // 4
            if which == 0:
                u = dict(q=QA[o:o + 64, j, :], k=KA[o:o + 64, j, :], v=lambda s, h=h: VA[:, s, h * 64:(h + 1) * 64],
                         bias=BIAS[:, h, :], need=[tq["qa"], tq["ka"], t_bias], needv=tq["va"])
            else:
                kk = (KS2, KW2)[which - 1]
                u = dict(q=QB[o:o + 64, j, :], k=kk[o:o + 64, g, :],
                         v=lambda s, g=g: VG[:, s, (which - 1) * 128 + g * 64:(which - 1) * 128 + g * 64 + 64],
                         bias=BIAS[:, 8 + h, :], need=[tq["qb"], dups[which - 1]], needv=tq["vg"])
            u.update(col=h * 64, slot=8 * which + h)
            us.append(u)
        return us

    GTv = GT.rearrange("p (a h c) -> p a h c", a=2, c=3)
    t_nsa = [None, None]

    def normalise(which, OB, tpv, tes):
        dn = DEN[:, 16 * which:16 * which + 16]
        rd = RD[:, 16 * which:16 * which + 16]
        k1 = V(lambda e: e.reciprocal(rd, dn), tes)
        rv = rd.rearrange("p (h a) -> p a h", a=2)
        if which:
            k1 = V(lambda e: e.tensor_tensor(rv, rv, GTv[:, :, :, which], ALU.mult), k1, tq["vg"])
        nt = []
        for a in range(2):
            cf = rv[:, a, :].unsqueeze(2).to_broadcast([128, 8, 64])
            src = P[OB[a]][:, :].rearrange("p (h d) -> p h d", h=8)
            if which < 2:
                dst = O[:, a, 0:512] if which == 0 else O[:, a, 512:1024]
                k = V(lambda e: e.tensor_tensor(dst.rearrange("p (h d) -> p h d", h=8), src, cf, ALU.mult), k1, tpv, t_tr)
                nt.append(k)
            else:
                k = V(lambda e: e.tensor_tensor(TM.rearrange("p (h d) -> p h d", h=8), src, cf, ALU.mult),
                      k1, tpv, t_htp, t_nsa[0], t_nsa[1])
                t_nsa[a] = V(lambda e: e.tensor_tensor(O[:, a, 512:1024], O[:, a, 512:1024], TM, ALU.add), k)
                nt.append(t_nsa[a])
            pf[OB[a]] = [k]
        return nt

    res = []
    att = attend(heads(1), LR, PR, PT, MX, DEN, (6, 7), res, [2], [3])
    dst = [copy_to(QA[:, 0:2, :], 0.125, "qa"), copy_to(QA[:, 2:4, :], 0.125, "qa"),
           copy_to(KA[:, 0:2, :], 1.0, "ka"), copy_to(KA[:, 2:4, :], 1.0, "ka")]
    for n in range(4):
        proj_cols(1, dst[n])
        run(att, 1)
        compress(n // 2, n % 2)
        if n == 2:
            compressed(0)
        run(att, 2 if n % 2 else 1)
    compressed(1)
    t_w1 = t_done[st["take"] - 1]
    run(att)
    t_nsa = normalise(1, (6, 7), *res)
    res = []
    att = attend(heads(2), LR, PR, PT, MX, DEN, (4, 5), res, [2], [3])
    cmp = compressed_attention()

    def some():
        for _ in range(3):
            run(att, 1)
            run(cmp, 1)
    run(att, 1)
    proj_rows(512, 2, evac_va, some)
    xt["free"] = t_done[st["take"] - 1]
    ring["over"] = list(range(8))
    some()
    run(cmp)
    run(att)
    normalise(2, (4, 5), *res)
    t_xo, t_tr2 = turn(tiles(O), [[t] * 2 for t in t_nsa], (0, 1), range(4, 8))
    t_xo = [None, t_xo[0]]
    res, acc = [], []
    att = attend(heads(0), LR, PR, PT, MX, DEN, (6, 7), res, [4], [5])
    proj = out_steps(t_xo, (2, 3, 0, 1), acc)
    run(att, 3)
    for n in range(4):
        run(proj, 1)
        run(att, 1 if n < 3 else 2)
    run(att)
    t_om = normalise(0, (6, 7), *res)
    t_xo2, t_tr = turn(tiles(O), [[t] * 2 for t in t_om], (4, 5), range(0, 4))
    t_xo[0] = t_xo2[0]
    t_tr = [t_tr, t_tr2]
    t_prev = t_nsa
    t_g = load_gains([2], t_xn)
    run(proj)
    t_acc = acc
    t_x = residual(t_acc, 1.0)
    arena["free"] = [t_tr]
    t_xn = rms(t_x, t_g, t_tr)
    t_xt, t_tr = turn(tiles(XN), t_xn)
    MK = ar(19968, 512, (("p (j m) -> p j m",), dict(j=2)))
    MV = ar(20480, 512, (("p (a c) -> p a c",), dict(a=2)))
    MEM = ar(3072, 2048, (("p (a n) -> p a n",), dict(a=2)))
    k_mem = dma(G, MEM, mem_in.rearrange("(a p) n -> p a n", p=128), s_mem, t_om, t_prev)
    t_g = load_gains([3], t_xn)
    t_acc = ffn(t_xt, lambda j: tq.setdefault("mem", turn(tiles(MEM), [[k_mem] * 2] * 2, (5, 7, 6, 4))) if j == 9 else None)
    t_x = residual(t_acc, 0.5)

    T.wait(tq["mem"][0])
    t_xn = rms(t_x, t_g, t_tr)
    proj_cols(1, lambda n, b, t: tq.setdefault("mk", [S(lambda e: e.activation(
        MK, P[b][:, :].rearrange("p (j m) -> p j m", j=2), ACT.Copy), t)]))
    proj_rows(256, 1, lambda a, b, t: [tq.setdefault(f"mv{a}", S(lambda e: e.activation(
        MV[:, a, :], P[b][:, 0:256], ACT.Copy), t))])
    xt["free"] = t_done[st["take"] - 1]

    t_xt, t_tr = turn(tiles(XN), t_xn)
    t_alpha["v"] = [G(lambda e, a=a: e.tensor_scalar(x[:, a, :], XN[:, a, :], 2 * ALPHA, None, ALU.mult), t_xn[a])
                    for a in range(2)]
    t_x = t_alpha["v"]
    arena["free"] = [t_x, t_tr]

    def mem_attention(MQ, t_mq, ocols, Pm, Tm, t_free, out_, rs, rp):
        us = []
        for h in range(4):
            o = 64 * (h % 2)
            us.append(dict(q=MQ[o:o + 64, h // 2, :], k=MK[o:o + 64, h // 2, :],
                           v=lambda s, h=h: MV[:, s, h * 64:(h + 1) * 64], bias=None,
                           need=[t_mq, tq["mk"]], needv=[tq["mv0"], tq["mv1"]], col=h * 64, slot=h, hold=[t_free]))
        res = []
        for _ in attend(us, Pm, Pm, Tm, MX, DEN, (6, 7), res, rs, rp):
            if not res:
                yield
        tpv, tes = res
        k1 = V(lambda e: e.reciprocal(DEN[:, 0:8], DEN[:, 0:8]), tes)
        for a in range(2):
            cf = DEN[:, 0:8].rearrange("p (h a) -> p a h", a=2)[:, a, :].unsqueeze(2).to_broadcast([128, 4, 64])
            k = V(lambda e, a=a, cf=cf: e.tensor_tensor(ocols[a].rearrange("p (h d) -> p h d", h=4),
                                                        P[6 + a][:, 0:256].rearrange("p (h d) -> p h d", h=4), cf, ALU.mult),
                  k1, tpv, t_free)
            pf[6 + a] = [k]
            out_.append(k)
        yield

    t_g = load_gains([4, 5], t_xn)
    t_acc = ffn(t_xt)
    t_x = norm_step(t_acc, 0.5, t_g)
    t_xt, t_tr = turn(tiles(x), t_x)
    scale_x(1.0, t_tr)

    SL_ = [ar(1536 * i, 1536) for i in range(13)]

    def pairs(t):
        return t.rearrange("p (j t) -> p j t", j=6)

    def rows(t):
        return t.rearrange("p (a n) -> p a n", a=2)

    gflat = gb[:, :, :].rearrange("p a n -> p (a n)")
    GUP, LORA, MQ = gflat[:, 0:768], gflat[:, 768:1536], gflat[:, 1536:2048].rearrange("p (j t) -> p j t", j=2)
    k_gup = dma(G, GUP, gup[:, :], s_gup, t_x)
    k_lora = dma(G, LORA, lora[:, :], s_lora, t_x)
    R, K, VT = pairs(SL_[0]), pairs(SL_[1]), pairs(SL_[7])
    LT = SL_[10].rearrange("p (j t) -> p j t", j=6)
    OM = sm[:, 192:212]
    OKA = sm[:, 212:218]
    WL = sm[:, 112:136]
    BON = sm[:, 136:160]
    t_om = G(lambda e: e.tensor_scalar(OM, vc[:, V_MU:V_MU + 20], -1.0, 1.0, ALU.mult, ALU.add), t_x, k_vec)
    t_oka = G(lambda e: e.tensor_scalar(OKA, vc[:, V_KA:V_KA + 6], -1.0, 1.0, ALU.mult, ALU.add), t_x, k_vec)
    tz = {}

    def shifted(dst, first, n, b, t):
        last, first_ = [], []
        for s in range(2):
            i = 2 * n + s
            d = dst[:, i, :]
            src = P[b][:, s * NT:(s + 1) * NT]
            om = OM[:, first + i:first + i + 1]
            first_.append(S(lambda e: e.activation(d, src, ACT.Copy, scale=om), t, t_om, t_acc))
        for s in range(2):
            i = 2 * n + s
            d = dst[:, i, :]
            src = P[b][:, s * NT:(s + 1) * NT]
            m = vc[:, V_MU + first + i:V_MU + first + i + 1]
            last.append(V(lambda e, d=d, src=src, m=m: e.scalar_tensor_tensor(
                out=d[:, 1:NT], in0=src[:, 0:NT - 1], scalar=m, in1=d[:, 1:NT], op0=ALU.mult, op1=ALU.add), *first_))
            tz[first + i] = last[-1]
        return last

    def evac_mq(n, b, t):
        tq["mq"] = [S(lambda e: e.activation(MQ, P[b][:, :].rearrange("p (j t) -> p j t", j=2), ACT.Copy, scale=0.125), t, t_x)]
        return tq["mq"]

    LD, A, Cc, KK, TP = (pairs(SL_[i]) for i in (3, 4, 5, 6, 11))
    SQ = pairs(SL_[12])
    t_ld, t_a, t_c, t_sq, t_rn = {}, {}, {}, {}, []
    t_mat, t_kr = {}, {}
    KR = AR[:, 8 * 1536:10 * 1536].rearrange("p (j c s t) -> p j c s t", j=6, c=4, s=2)

    def ch(t):
        return t.rearrange("p (c t) -> p c t", c=4)

    def squares(j):
        t_sq[j] = S(lambda e: e.activation(SQ[:, j, :], K[:, j, :], ACT.Square, scale=vc[:, V_KK + j:V_KK + j + 1]),
                    tz[6 + j], k_vec)

    SEL, SPREAD = SL_[11][:, 0:72], SL_[11][0:12, 72:840]
    NRM = [SL_[11][0:12, 840:1096], SL_[11][0:12, 1152:1408]]
    k_sel = dma(G, SL_[11][:, 0:840], cst[:, C_SEL:C_ALL], s_sel, t_acc)

    def summed(j):
        if j == 0:
            T.wait(*pf[5])
        T.wait(t_sq[j], k_sel)
        mm(P[5][0:12, 0:NT], SEL[:, 12 * j:12 * j + 12], SQ[:, j, :], j == 0, j == 5)

    def roots():
        t = T.mark()
        t1 = V(lambda e: e.tensor_scalar(NRM[0], P[5][0:12, 0:NT], 1e-24, None, ALU.max), t)
        pf[5] = [t1]
        t2 = S(lambda e: e.activation(NRM[1], NRM[0], ACT.Sqrt), t1)
        return V(lambda e: e.reciprocal(NRM[0], NRM[1]), t2)

    def normed(n):
        b = bank()
        T.wait(t_root)
        for i in range(2):
            j = 2 * n + i
            mm(P[b][:, i * NT:(i + 1) * NT], SPREAD[:, 128 * j:128 * j + 128], NRM[0])
        t = T.mark()
        for i in range(2):
            j = 2 * n + i
            kk_ = vc[:, V_KK + j:V_KK + j + 1]
            t_rn.append(V(lambda e: e.scalar_tensor_tensor(out=KK[:, j, :], in0=K[:, j, :], scalar=kk_,
                                                           in1=P[b][:, i * NT:(i + 1) * NT],
                                                           op0=ALU.mult, op1=ALU.mult), t))
        pf[b] = [t_rn[-1]]

    def low_rank(j):
        b, b2 = bank(), bank()
        T.wait(t_th, tz[18], k_lora)
        mm(P[b][:, 0:NT], LORA[0:64, j * 128:(j + 1) * 128], LT[0:64, 0, :])
        mm(P[b2][:, 0:NT], LORA[64:128, j * 128:(j + 1) * 128], LT[64:128, 0, :])
        t = T.mark()
        t1 = S(lambda e: e.activation(LD[:, j, :], P[b][:, 0:NT], ACT.Sigmoid, bias=vc[:, V_W0 + j:V_W0 + j + 1]), t)
        t2 = S(lambda e: e.activation(A[:, j, :], P[b2][:, 0:NT], ACT.Sigmoid, bias=vc[:, V_A0 + j:V_A0 + j + 1]), t)
        pf[b], pf[b2] = [t1], [t2]
        t_ld[j] = G(lambda e: e.tensor_scalar(LD[:, j, :], LD[:, j, :], -DECAY, None, ALU.mult), t1)
        t_a[j] = t2
        return t

    def keys(j):
        ka, ok = vc[:, V_KA + j:V_KA + j + 1], OKA[:, j:j + 1]
        rk = vc[:, V_RK + j:V_RK + j + 1]
        t_c[j] = V(lambda e: e.tensor_tensor_scan(Cc[:, j, :], cs[:, C_SCAN:C_SCAN + NT], LD[:, j, :], 0.0,
                                                  ALU.mult, ALU.add), t_ld[j], k_cst)
        t1 = V(lambda e: e.tensor_scalar(TP[:, j, :], A[:, j, :], ka, ok, ALU.mult, ALU.add), t_a[j], t_oka, t_rn)
        t2 = V(lambda e: e.tensor_tensor(K[:, j, :], K[:, j, :], TP[:, j, :], ALU.mult), t1)
        t3 = V(lambda e: e.scalar_tensor_tensor(out=SQ[:, j, :], in0=R[:, j, :], scalar=rk, in1=K[:, j, :],
                                                op0=ALU.mult, op1=ALU.mult), t2, tz[j], t_rn)
        t4 = G(lambda e: e.tensor_tensor(A[:, j, :], A[:, j, :], KK[:, j, :], ALU.mult), t1, t_rn)
        t_k[j], t_sq[j], t_a[j] = t2, t3, t4

    def decayed(j):
        t1 = S(lambda e: e.activation(TP[:, j, :], Cc[:, j, :], ACT.Exp, scale=-1.0), t_c[j], t_k[j])
        t2 = V(lambda e: e.tensor_tensor(A[:, j, :], A[:, j, :], TP[:, j, :], ALU.mult), t1, t_a[j])
        t3 = V(lambda e: e.tensor_tensor(K[:, j, :], K[:, j, :], TP[:, j, :], ALU.mult), t1, t_k[j], t_sq[j])
        t4 = G(lambda e: e.tensor_tensor(LD[:, j, :], Cc[:, j, :], LD[:, j, :], ALU.subtract), t_c[j])
        t5 = S(lambda e: e.activation(Cc[:, j, :], Cc[:, j, :], ACT.Exp), t1, t4)
        t6 = S(lambda e: e.activation(LD[:, j, :], LD[:, j, :], ACT.Exp), t4)
        t7 = V(lambda e: e.tensor_tensor(KR[:, j, :, 1, :], ch(R[:, j, :]), ch(Cc[:, j, :]), ALU.mult), t5, tz[j])
        t8 = V(lambda e: e.tensor_tensor(KR[:, j, :, 0, :], ch(KK[:, j, :]), ch(LD[:, j, :]), ALU.mult), t6, t_rn)
        t9 = G(lambda e: e.tensor_copy(WL[:, 4 * j:4 * j + 4], Cc[:, j, 63:NT:64]), t5)
        t_mat[j] = [t2, t3]
        t_kr[j] = [t7, t8, t9]

    T.wait(t_xt)
    ring["over"] = [0, 1, 2, 3]
    t_k = {}
    for n in range(3):
        proj_cols(1, lambda _, b, t: shifted(K, 6, n, b, t))
        squares(2 * n)
        squares(2 * n + 1)
        if n:
            summed(2 * n - 2)
            summed(2 * n - 1)
    proj_cols(1, lambda n, b, t: shifted(LT, 18, n, b, t))
    summed(4)
    summed(5)
    t_root = roots()
    t_th = S(lambda e: e.activation(LT[0:64, 0, :], LT[0:64, 0, :], ACT.Tanh), tz[18])
    t_dg = S(lambda e: e.activation(LT[:, 1, :], LT[:, 1, :], ACT.Sigmoid), tz[19])
    for n in range(3):
        proj_cols(1, lambda _, b, t: shifted(R, 0, n, b, t))
        if n == 0:
            for i in range(3):
                normed(i)
        if n:
            keys(2 * n - 2)
            keys(2 * n - 1)
        low_rank(2 * n)
        t_lora = low_rank(2 * n + 1)
    DGK = gflat[:, 768:1024]
    proj_cols(1, evac_mq)
    keys(4)
    keys(5)
    t_dg2 = S(lambda e: e.activation(DGK, LT[:, 1, :], ACT.Copy), t_dg, t_lora)
    t_memo = []
    W = [SL_[2][:, 512 * i:512 * i + 512] for i in range(3)] + [SL_[10][:, 512:1024]]
    att = mem_attention(MQ, tq["mq"], [gflat[:, 1536:1792], gflat[:, 1792:2048]], W[0:2], W[2:4], [t_acc], t_memo, [4], [5])
    run(att, 1)
    decayed(0)
    for n in range(3):
        proj_cols(1, lambda _, b, t: shifted(VT, 12, n, b, t))
        run(att, 1)
        decayed(2 * n + 1)
        run(att, 1)
        if n < 2:
            decayed(2 * n + 2)
    run(att)
    xt["free"] = t_done[st["take"] - 1]
    ring["over"] = list(range(8))
    t_r = [tz[i] for i in range(6)]
    t_c, t_sq, t_a, t_mat, t_kr = (list(t.values()) for t in (t_c, t_sq, t_a, t_mat, t_kr))
    Vt = rows(SL_[2])

    def by_tokens(src, dst, toks, free=None):
        res = []
        for a in range(2):
            for lo_, w in ((0, 4), (4, 2)):
                b = bank()
                T.wait(*toks)
                for j in range(w):
                    tr(P[b][:, j * 128:(j + 1) * 128], src[:, lo_ + j, a * 128:(a + 1) * 128])
                t = T.mark()
                o, i = dst[:, a, lo_ * 128:(lo_ + w) * 128], P[b][:, 0:w * 128]
                if w == 4:
                    k = S(lambda e, o=o, i=i: e.activation(o, i, ACT.Copy), t, free)
                else:
                    k = V(lambda e, o=o, i=i: e.tensor_copy(o, i), t, free)
                pf[b] = [k]
                res.append(k)
        return res, t

    t_vt, t_vtp = by_tokens(VT, Vt, [tz[12 + j] for j in range(6)], t_memo)
    b = bank()
    T.wait(t_sq)
    for a in range(2):
        for j in range(6):
            c = a * 12 + 2 * j
            mm(P[b][:, c:c + 2], SQ[:, j, a * 128:(a + 1) * 128], cs[:, C_BLK2:C_BLK2 + 2])
    t = T.mark()
    t_bon = V(lambda e: e.tensor_copy(BON, P[b][:, 0:24]), t)
    pf[b] = [t_bon]
    t_bonp = t
    def blocks(t):
        return t.rearrange("p (q h t) -> p q h t", q=2, h=12)

    AT, CT_, RBT, RKT, X, XT, T1, AM = (blocks(SL_[i]) for i in (5, 6, 7, 12, 10, 11, 4, 1))
    def flat(t):
        return t.rearrange("p q h t -> p (q h) t")

    t_at, t_ct, t_rb, t_rk = {}, {}, {}, {}
    ring["over"] = list(range(7))
    T.wait(*pf[7])
    warm(16)
    for g in range(3):
        for what in range(2):
            for hb in range(2):
                src, d0, d1 = ((A, AT, RBT), (K, CT_, RKT))[what]
                b = bank()
                T.wait(t_mat, t_kr, t_vtp, t_bonp)
                o = 64 * hb
                for i in range(4):
                    q, j = divmod(4 * g + i, 6)
                    for p in range(2):
                        c = 2 * q + p
                        mm(P[b][64 * p:64 * p + 64, i * 128:(i + 1) * 128], src[o:o + 64, j, c * 64:(c + 1) * 64],
                           KR[o:o + 64, j, c, :, :].rearrange("p s t -> p (s t)"))
                warm(1)
                t = T.mark()
                pv = P[b][:, :].rearrange("p (h s t) -> p h s t", h=4, s=2)
                m0 = cs[:, C_MLT:C_MLT + 64].unsqueeze(1).to_broadcast([128, 4, 64])
                m1 = cs[:, C_MLE:C_MLE + 64].unsqueeze(1).to_broadcast([128, 4, 64])
                at_ = slice(8 * g + hb, 8 * g + 8, 2)
                t1 = V(lambda e: e.tensor_tensor(flat(d0)[:, at_, :], pv[:, :, 0, :], m0, ALU.mult), t, t_kr, t_dg2)
                t2 = V(lambda e: e.tensor_tensor(flat(d1)[:, at_, :], pv[:, :, 1, :], m1, ALU.mult), t, t_kr)
                pf[b] = [t1, t2]
                (t_at, t_ct)[what][(g, hb)] = t1
                (t_rb, t_rk)[what][(g, hb)] = t2
    t_prod = t
    Bt, Kt = rows(SL_[0]), rows(SL_[3])
    t_bt, _ = by_tokens(A, Bt, [t_mat[j][0] for j in range(6)], t_kr)
    t_kt, t_turned = by_tokens(K, Kt, [t_mat[j][1] for j in range(6)], t_kr)
    fAT, fX, fXT, fT1, fAM = (flat(t) for t in (AT, X, XT, T1, AM))
    i64 = cs[:, C_I64:C_I64 + 64].unsqueeze(1).to_broadcast([128, 8, 64])
    t_all_at = list(t_at.values())
    tx, txt, tam, tam_free = {}, {}, {}, {}
    gs = [slice(8 * g, 8 * g + 8) for g in range(3)]

    def level_mask(l, g):
        m = cs[:, C_LEV + 64 * l:C_LEV + 64 * l + 64].unsqueeze(1).to_broadcast([128, 8, 64])
        tam[g] = G(lambda e: e.tensor_tensor(fAM[:, gs[g], :], fAT[:, gs[g], :], m, ALU.mult),
                   t_all_at, t_turned, t_prod, tam_free.get(g), t_bonp)

    def group_mm(b, g, l, r):
        for p in range(2):
            warm(1)
            for i in range(8):
                mm(P[b][64 * p:64 * p + 64, i * 64:(i + 1) * 64], l[64 * p:64 * p + 64, 8 * g + i, :], r(p, i))

    warm(8)
    for g in range(3):
        level_mask(0, g)
        txt[g] = V(lambda e, g=g: e.tensor_tensor(fXT[:, gs[g], :], i64, fAM[:, gs[g], :], ALU.subtract), tam[g], t_mat)
    for g in range(3):
        b = bank()
        T.wait(tam[g])
        group_mm(b, g, fAM, lambda p, i: cs[64 * p:64 * p + 64, C_I64:C_I64 + 64])
        t = T.mark()
        tx[g] = V(lambda e, g=g, b=b: e.tensor_tensor(fX[:, gs[g], :], i64, P[b][:, :].rearrange("p (i t) -> p i t", i=8),
                                                      ALU.subtract), t, t_dg2)
        pf[b] = [tx[g]]
        tam_free[g] = [t, txt[g]]
    for l in range(1, 6):
        t1s = {}
        for g in range(3):
            level_mask(l, g)
        for g in range(3):
            b = bank()
            T.wait(tam[g], tx[g])
            group_mm(b, g, fAM, lambda p, i, g=g: fX[64 * p:64 * p + 64, 8 * g + i, :])
            t = T.mark()
            tam_free[g] = t
            t1s[g] = S(lambda e, g=g, b=b: e.activation(fT1[:, gs[g], :], P[b][:, :].rearrange("p (i t) -> p i t", i=8),
                                                        ACT.Copy), t, t_turned, t_prod, txt[g])
            pf[b] = [t1s[g]]
        for g in range(3):
            T.wait(t1s[g], txt[g])
            ps = []
            if l < 5:
                b = bank()
                group_mm(b, g, fXT, lambda p, i, g=g: fT1[64 * p:64 * p + 64, 8 * g + i, :])
                ps.append(b)
            b3 = bank()
            group_mm(b3, g, fT1, lambda p, i, g=g: fXT[64 * p:64 * p + 64, 8 * g + i, :])
            t = T.mark()
            if ps:
                tx[g] = V(lambda e, g=g, b=ps[0]: e.tensor_tensor(fX[:, gs[g], :], fX[:, gs[g], :],
                                                                  P[b][:, :].rearrange("p (i t) -> p i t", i=8),
                                                                  ALU.subtract), t)
                pf[ps[0]] = [tx[g]]
            txt[g] = V(lambda e, g=g, b=b3: e.tensor_tensor(fXT[:, gs[g], :], fXT[:, gs[g], :],
                                                            P[b][:, :].rearrange("p (i t) -> p i t", i=8),
                                                            ALU.subtract), t)
            pf[b3] = [txt[g]]
    t_inv = list(txt.values())
    t_invp = t
    RH, UU = SL_[4][:, 0:768], SL_[4][:, 768:1536]
    STT = [SL_[1][:, 384 * i:384 * (i + 1)].rearrange("p (j n) -> p j n", j=6) for i in range(2)]
    STM = SL_[1][:, 768:1152].rearrange("p (j n) -> p j n", j=6)
    OUT = rows(SL_[10])
    CV, GK = rows(SL_[5]), rows(SL_[6])
    WLv = WL.rearrange("p (j c) -> p j c", j=6)

    def heads_of(bb, o):
        return lambda h: P[bb[h // 8]][o:o + 64, (h % 8) * 64:(h % 8) * 64 + 64]

    def parity(bb, o):
        return lambda h: P[bb[h % 2]][o:o + 64, (h // 2) * 64:(h // 2) * 64 + 64]

    def of_parity(t, i):
        return t.rearrange("p (j b d) -> p j b d", j=6, b=2)[:, :, i, :]

    def head_cols(t, h):
        return t[:, h * 64:(h + 1) * 64]

    def six(b, o):
        return P[b][o:o + 64, 0:384].rearrange("p (j d) -> p j d", j=6)

    t_cv = []
    for q in range(2):
        bb = [bank(), bank()]
        T.wait(list(t_ct.values()), t_vt)
        for h in range(12):
            for o in (0, 64):
                mm(heads_of(bb, o)(h), CT_[o:o + 64, q, h, :], head_cols(Vt[o:o + 64, q, :], h))
        t = T.mark()
        for i, (lo_, w) in enumerate(((0, 512), (512, 256))):
            k = S(lambda e: e.activation(CV[:, q, lo_:lo_ + w], P[bb[i]][:, 0:w], ACT.Copy, scale=-1.0), t, list(tam.values()))
            pf[bb[i]] = [k]
            t_cv.append(k)
    t_cvp = t
    t_gk = []
    for a in range(2):
        bb = [bank(), bank()]
        T.wait(t_dg2, k_gup)
        mm(P[bb[0]][:, :], DGK[:, a * 128:(a + 1) * 128], GUP[:, 0:512])
        mm(P[bb[1]][:, 0:256], DGK[:, a * 128:(a + 1) * 128], GUP[:, 512:768])
        t = T.mark()
        k1 = S(lambda e: e.activation(GK[:, a, 0:512], P[bb[0]][:, :], ACT.Copy), t, t_cvp)
        k2 = S(lambda e: e.activation(GK[:, a, 512:768], P[bb[1]][:, 0:256], ACT.Copy), t, t_cvp)
        pf[bb[0]], pf[bb[1]] = [k1], [k2]
        t_gk += [k1, k2]
    t_gp = t
    k_lnx = dma(G, gflat[:, 0:1536], bass.AP(lnx.tensor, 0, [[0, 128], [1, 1536]]), s_lnx, t_gp, t_th)

    def wide(t):
        return t.unsqueeze(2).to_broadcast([128, 12, 64])

    BO = [SL_[0][:, 0:768], SL_[3][:, 0:768]]
    SQR = SL_[7][:, 0:768]
    t_bo = []

    def bonuses(t_half):
        for a in range(2):
            bov, vv = (t.rearrange("p (h d) -> p h d", h=12) for t in (BO[a], Vt[:, a, :]))
            bon = wide(BON[:, a * 12:(a + 1) * 12])
            g1 = G(lambda e: e.tensor_tensor(bov, vv, bon, ALU.mult), t_bon, t_vt, t_half)
            g2 = G(lambda e: e.tensor_tensor(BO[a], BO[a], gflat[:, 768:1536], ALU.add), g1, k_lnx)
            g3 = G(lambda e: e.tensor_tensor(BO[a], BO[a], GK[:, a, :], ALU.mult), g2, t_gk)
            g4 = G(lambda e: e.tensor_tensor(GK[:, a, :], GK[:, a, :], gflat[:, 0:768], ALU.mult), g3)
            t_bo.append([g3, g4])

    MEAN, VAR = sm[:, 48:72], sm[:, 72:96]
    t_heads = [None, None]

    def group_norm(a):
        ov = OUT[:, a, :].rearrange("p (h d) -> p h d", h=12)
        sqv = SQR.rearrange("p (h d) -> p h d", h=12)
        mean, var = MEAN[:, a * 12:(a + 1) * 12], VAR[:, a * 12:(a + 1) * 12]
        t1 = V(lambda e: e.tensor_reduce(mean, ov, AX.X, ALU.add), tq["out"], t_memo)
        t2 = V(lambda e: e.tensor_scalar(mean, mean, 1.0 / 64, None, ALU.mult), t1)
        yield
        t3 = V(lambda e: e.tensor_tensor(ov, ov, wide(mean), ALU.subtract), t2)
        t4 = S(lambda e: e.activation(sqv, ov, ACT.Square), t3, tq.get("sqr"), t_or)
        yield
        tq["sqr"] = t5 = V(lambda e: e.tensor_reduce(var, sqv, AX.X, ALU.add), t4)
        t6 = V(lambda e: e.tensor_scalar(var, var, 1.0 / 64, 64e-5, ALU.mult, ALU.add), t5)
        t7 = S(lambda e: e.activation(var, var, ACT.Sqrt), t6)
        yield
        t8 = V(lambda e: e.reciprocal(var, var), t7)
        t9 = V(lambda e: e.tensor_tensor(ov, ov, wide(var), ALU.mult), t8)
        yield
        t10 = V(lambda e: e.tensor_tensor(OUT[:, a, :], OUT[:, a, :], GK[:, a, :], ALU.mult), t9, t_bo[a])
        yield
        t_heads[a] = [V(lambda e: e.tensor_tensor(OUT[:, a, :], OUT[:, a, :], BO[a], ALU.add), t10), t_memo]
        yield

    gn = iter(())
    t_st, t_or = None, []
    need0 = [t_inv, list(t_rb.values()), list(t_rk.values()), t_bt, t_kt, t_vt]
    for c in range(4):
        q, p = c // 2, c % 2
        o = 64 * p
        sc, sn = STT[c % 2], STT[(c + 1) % 2]
        cv = CV[o:o + 64, q, :]
        if c == 2:
            bonuses(t_or)
            gn = group_norm(0)
        T.wait(need0)
        if c:
            bb = [bank(), bank()]
            warm(3)
            T.wait(t_st)
            for h in range(12):
                ho, j = 64 * (h % 2), h // 2
                mm(parity(bb, o)(h), KR[ho:ho + 64, j, c, 0, :], sc[ho:ho + 64, j, :])
            t = T.mark()
            t1 = []
            for i in range(2):
                k = V(lambda e: e.tensor_tensor(of_parity(RH[o:o + 64, :], i), of_parity(cv, i), six(bb[i], o), ALU.subtract),
                      t, t_cv, t_invp)
                pf[bb[i]] = [k]
                t1.append(k)
            run(gn, 1)
            rh = RH[o:o + 64, :]
        else:
            t1, rh = t_cv, cv
        bb = [bank(), bank()]
        warm(3)
        T.wait(t1)
        for h in range(12):
            mm(heads_of(bb, o)(h), XT[o:o + 64, q, h, :], head_cols(rh, h))
        t = T.mark()
        uu = UU[o:o + 64, :]
        t1 = V(lambda e: e.tensor_copy(uu[:, 0:512], P[bb[0]][o:o + 64, :]), t, t_invp)
        t2 = S(lambda e: e.activation(uu[:, 512:768], P[bb[1]][o:o + 64, 0:256], ACT.Copy), t, t_invp)
        pf[bb[0]], pf[bb[1]] = [t1], [t2]
        warm(3)
        T.wait(t1, t2)
        vt = Vt[o:o + 64, q, :]
        if c < 3:
            b = bank()
            for h in range(12):
                ho, j = 64 * (h % 2), h // 2
                d = P[b][ho:ho + 64, j * 64:(j + 1) * 64]
                mm(d, head_cols(Bt[o:o + 64, q, :], h), head_cols(uu, h), True, False)
                mm(d, head_cols(Kt[o:o + 64, q, :], h), head_cols(vt, h), False, True)
            t = T.mark()
            wl = WLv[:, :, c].unsqueeze(2).to_broadcast([128, 6, 64])
            pv = P[b][:, 0:384].rearrange("p (j n) -> p j n", j=6)
            if c:
                t3 = V(lambda e: e.tensor_tensor(STM, pv, sc, ALU.add), t, t_st)
                t_st = V(lambda e: e.tensor_tensor(sn, STM, wl, ALU.mult), t3, t_or)
            else:
                t3 = t_st = V(lambda e: e.tensor_tensor(sn, pv, wl, ALU.mult), t, t_invp)
            pf[b] = [t3]
        run(gn, 1)
        bb = [bank(), bank()]
        for h in range(12):
            d = heads_of(bb, o)(h)
            mm(d, RBT[o:o + 64, q, h, :], head_cols(uu, h), True, False)
            mm(d, RKT[o:o + 64, q, h, :], head_cols(vt, h), False, True)
        t = T.mark()
        ot = OUT[o:o + 64, q, :]
        t1 = S(lambda e: e.activation(ot[:, 0:512], P[bb[0]][o:o + 64, :], ACT.Copy), t, t_invp)
        t2 = S(lambda e: e.activation(ot[:, 512:768], P[bb[1]][o:o + 64, 0:256], ACT.Copy), t, t_invp)
        pf[bb[0]], pf[bb[1]] = [t1], [t2]
        res = [t1, t2]
        if c:
            bb = [bank(), bank()]
            for h in range(12):
                ho, j = 64 * (h % 2), h // 2
                mm(parity(bb, o)(h), KR[ho:ho + 64, j, c, 1, :], sc[ho:ho + 64, j, :])
            t = T.mark()
            for i in range(2):
                k = V(lambda e: e.tensor_tensor(of_parity(ot, i), of_parity(ot, i), six(bb[i], o), ALU.add), t, t1, t2)
                pf[bb[i]] = [k]
                res.append(k)
        t_or = [t]
        run(gn, 1)
        tq.setdefault("out", []).extend(res)
    run(gn)
    run(group_norm(1))
    ring["over"] = list(range(8))
    xt["free"] = [t_or, t_heads]
    def heads_tiles(a, k):
        if k < 6:
            return OUT[:, a, k * 128:(k + 1) * 128]
        return gflat[:, 1536 + a * 256 + (k - 6) * 128:1536 + a * 256 + (k - 5) * 128]

    t_xt, t_tr = turn(heads_tiles, t_heads, by_quarter=False)
    t_g = load_gains([6, 7], t_tr)
    t_acc = out_proj(t_xt)
    t_x = norm_step(t_acc, 1.0, t_g)
    arena["free"] = [t_tr]
    t_xt, t_tr = turn(tiles(x), t_x)
    scale_x(0.5, t_tr)
    t_g = load_gains([8, 9], t_x)
    t_acc = ffn(t_xt)
    t_x = norm_step(t_acc, 0.5, t_g)
    t_xt, t_tr = turn(tiles(x), t_x)
    scale_x(0.5, t_tr)

    t_g = load_gains([10, 11], t_x)
    t_acc = ffn(t_xt)
    t_x = norm_step(t_acc, 0.5, t_g)
    t_xt, t_tr = turn(tiles(x), t_x)
    scale_x(1.0, t_tr)
    Q, K2, VS = pairs(SL_[0]), pairs(SL_[1]), rows(SL_[2])
    tk = {"q": [], "k": [], "v": []}

    def evac_qk(dst, scale, key):
        def evac(n, b, t):
            o = dst[:, 2 * n:2 * n + 2, :]
            src = P[b][:, :].rearrange("p (s t) -> p s t", s=2)
            if n % 2 == 0:
                k = S(lambda e: e.activation(o, src, ACT.Copy, scale=scale), t, t_acc)
            else:
                k = V(lambda e: e.tensor_scalar(o, src, scale, None, ALU.mult), t, t_acc)
            tk[key].append(k)
            return [k]
        return evac

    def evac_v(o, w):
        def evac(a, b, t):
            k = S(lambda e: e.activation(VS[:, a, o:o + w], P[b][:, 0:w], ACT.Copy), t, t_acc)
            tk["v"].append(k)
            return [k]
        return evac

    MN, MB_ = SL_[3][:, 0:384], SL_[3][:, 384:768]
    keep, neg = cs[:, C_KEEP:C_KEEP + 128], cs[:, C_NEG:C_NEG + 128]
    t_m = []
    for o in (0, 256):
        t_m.append(G(lambda e, o=o: e.tensor_scalar(MN[:, o:o + 128], keep, -1.0, None, ALU.mult), t_acc))
        t_m.append(G(lambda e, o=o: e.tensor_copy(MB_[:, o:o + 128], neg), t_acc))
    t_m.append(G(lambda e: e.memset(MN[:, 128:256], -1.0), t_acc))
    t_m.append(G(lambda e: e.memset(MB_[:, 128:256], 0.0), t_acc))
    W3 = AR[:, 4 * 1536:10 * 1536].rearrange("p (i n) -> p i n", n=384)
    NA, LK, EE = ([W3[:, 8 * i + j, :] for j in range(8)] for i in range(3))
    zb = {}
    tZ, tN, tL, tK, tE2, tA, tX, tP = {}, {}, {}, {}, {}, {}, {}, {}
    OUT = rows(SL_[10])

    def qk(b, h, s, stop_):
        o, j = 64 * (h % 2), h // 2
        d, q0 = ((0, 0), (256, 128))[s]
        mm(P[b][:, d:d + NT - q0], K2[o:o + 64, j, s * 128:(s + 1) * 128], Q[o:o + 64, j, q0:NT], True, stop_)

    def st_a(h, b):
        zb[h] = b
        T.wait(*pf[b], tk["q"], tk["k"])
        qk(b, h, 0, True)
        qk(b, h, 1, True)
        tZ[h] = T.mark()
        r = h % 8
        tN[h] = S(lambda e: e.activation(NA[r], P[b][:, 0:384], ACT.Abs), tZ[h], tK.get(h - 8), t_acc)
        tN[h] = S(lambda e: e.activation(NA[r], NA[r], ACT.Exp, scale=-1.0), tN[h])

    def st_l(h):
        b, r = zb[h], h % 8
        tL[h] = S(lambda e: e.activation(NA[r], NA[r], ACT.Ln, bias=1.0, scale=1.0), tN[h])
        t1 = V(lambda e: e.scalar_tensor_tensor(out=LK[r], in0=P[b][:, 0:384], scalar=0.0, in1=NA[r],
                                                op0=ALU.max, op1=ALU.add), tL[h], tE2.get(h - 8))
        tK[h] = V(lambda e: e.tensor_tensor(LK[r], LK[r], MN, ALU.mult), t1, t_m)

    def st_b(h):
        b, r = zb[h], h % 8
        T.wait(tK[h], tN[h], k_cst)
        tri, ones = cs[:, C_TRI:C_TRI + 128], cs[:, C_ONES:C_ONES + 128]
        qk(b, h, 0, False)
        mm(P[b][:, 0:256], tri, LK[r][:, 0:256], False, False)
        mm(P[b][:, 128:256], ones, LK[r][:, 256:384], False, True)
        qk(b, h, 1, False)
        mm(P[b][:, 256:384], tri, LK[r][:, 256:384], False, True)
        tE2[h] = T.mark()

    def st_c(h):
        b, r = zb[h], h % 8
        tA[h] = V(lambda e: e.tensor_tensor(EE[r], P[b][:, 0:384], MB_, ALU.add), tE2[h], tP.get(h - 8), t_m)
        pf[b] = [tA[h]]
        tX[h] = S(lambda e: e.activation(EE[r], EE[r], ACT.Exp), tA[h])

    def st_d(h):
        r = h % 8
        T.wait(tX[h], tk["v"])
        if h in (0, 8):
            T.wait(pf[6], pf[7])
        c = (h % 8) * 64
        v = [VS[:, s, h * 64:(h + 1) * 64] for s in range(2)]
        mm(P[6][:, c:c + 64], EE[r][:, 0:128], v[0])
        mm(P[7][:, c:c + 64], EE[r][:, 128:256], v[0], True, False)
        mm(P[7][:, c:c + 64], EE[r][:, 256:384], v[1], False, True)
        tP[h] = T.mark()
        if h in (7, 11):
            o, w = (0, 512) if h == 7 else (512, 256)
            t_hd2.append([])
            for a in range(2):
                if a:
                    k = V(lambda e: e.tensor_copy(OUT[:, a, o:o + w], P[6 + a][:, 0:w]), tP[h], t_acc)
                else:
                    k = S(lambda e: e.activation(OUT[:, a, o:o + w], P[6 + a][:, 0:w], ACT.Copy), tP[h], t_acc)
                pf[6 + a] = [k]
                t_hd2[-1].append(k)

    t_hd2, t_memo = [], []
    W = [AR[:, 11 * 1536 + 512 * i:11 * 1536 + 512 * i + 512] for i in range(6)]
    T.wait(t_xt)
    ring["over"] = [0, 1]
    proj_cols(1, evac_mq)
    att = mem_attention(MQ, tq["mq"], [gflat[:, 1536:1792], gflat[:, 1792:2048]], W[0:3], W[3:6], [t_acc], t_memo, [2], [3])
    run(att, 1)
    proj_cols(1, evac_qk(Q[:, 0:2, :], 0.125, "q"))
    run(att, 1)
    proj_cols(1, evac_qk(K2[:, 0:2, :], 1.0, "k"))
    run(att, 1)
    proj_rows(512, 2, evac_v(0, 512), lambda: run(att, 2))
    run(att)
    def each(part, hs, *bb):
        for i, h in enumerate(hs):
            part(h, *[b[i] for b in bb])

    h0, h1, h2, h3 = range(0, 4), range(4, 8), range(8, 10), range(10, 12)
    each(st_a, h0, (2, 3, 4, 5))
    proj_cols(1, evac_qk(Q[:, 2:4, :], 0.125, "q"))
    each(st_l, h0)
    proj_cols(1, evac_qk(K2[:, 2:4, :], 1.0, "k"))
    each(st_b, h0)
    each(st_c, h0)
    proj_cols(1, evac_qk(Q[:, 4:6, :], 0.125, "q"))
    each(st_a, h1, (2, 3, 4, 5))
    each(st_d, h0)
    proj_cols(1, evac_qk(K2[:, 4:6, :], 1.0, "k"))
    each(st_l, h1)
    proj_rows(256, 1, evac_v(512, 256))
    xt["free"] = t_done[st["take"] - 1]
    ring["over"] = list(range(8))
    each(st_b, h1)
    each(st_c, h1)
    each(st_a, h2, (4, 5))
    each(st_d, h1)
    t_xo, t_tr2 = turn(heads_tiles, [[t] for t in t_hd2[0]], (0, 1), range(0, 4))
    t_xo = [t_xo[0], None]
    acc = []
    proj = out_steps(t_xo, (0, 1, 2, 3), acc)
    each(st_l, h2)
    run(proj, 1)
    each(st_b, h2)
    each(st_c, h2)
    each(st_a, h3, (4, 5))
    run(proj, 1)
    each(st_d, h2)
    each(st_l, h3)
    run(proj, 1)
    each(st_b, h3)
    each(st_c, h3)
    run(proj, 1)
    each(st_d, h3)
    t_heads = [[t_hd2[1][a], t_memo] for a in range(2)]
    t_xo[1], t_tr = turn(heads_tiles, t_heads, (4, 5), range(4, 8), by_quarter=False)
    t_xo[1] = t_xo[1][0]
    t_tr = [t_tr, t_tr2]
    t_g = load_gains([12, 13], t_tr)
    run(proj)
    t_acc = acc
    t_x = norm_step(t_acc, 1.0, t_g)
    arena["free"] = [t_tr]
    t_xt, t_tr = turn(tiles(x), t_x)
    scale_x(0.5, t_tr)
    t_g = load_gains([14, 15], t_x)
    t_acc = ffn(t_xt)
    t_x = norm_step(t_acc, 0.5, t_g)
    t_out = dma(Y, out.rearrange("(a p) n -> p a n", p=128), x[:, :, :], s_out, t_x)
    Y.wait(t_out, list(sent.values()))


def build(nc, *aps):
    with ExitStack() as ctx:
        program(nc, ctx, *aps)


def constants():
    p = np.arange(128)
    c = np.zeros((128, C_ALL), np.float32)
    c[:, C_ID:C_ID + 128] = np.eye(128)
    c[:, C_TRI:C_TRI + 128] = p[:, None] >= p[None, :]
    keep = (p[None, :] > p[:, None]).astype(np.float32)
    c[:, C_KEEP:C_KEEP + 128] = keep
    c[:, C_NEG:C_NEG + 128] = (keep - 1) * BIG
    c[:, C_BLK:C_BLK + 128] = p[:, None] // 64 == p[None, :] // 64
    c[:, C_BLK2:C_BLK2 + 2] = p[:, None] // 64 == np.arange(2)[None, :]
    s, t = (p % 64)[:, None], np.arange(64)[None, :]
    c[:, C_MLT:C_MLT + 64] = s < t
    c[:, C_MLE:C_MLE + 64] = s <= t
    for l in range(6):
        m = 1 << l
        c[:, C_LEV + 64 * l:C_LEV + 64 * l + 64] = (s // (2 * m) == t // (2 * m)) & (s // m % 2 == 0) & (t // m % 2 == 1)
    c[:, C_SCAN:C_SCAN + NT] = np.arange(NT)[None, :] % 64 != 0
    c[:, C_I64:C_I64 + 64] = s == t
    c[:, C_ONES:C_ONES + 128] = 1
    c[:, C_FLIP:C_FLIP + 128] = np.eye(128)[::-1]
    for j in range(6):
        for i in range(2):
            c[64 * i:64 * i + 64, C_SEL + 12 * j + 2 * j + i] = 1
            c[2 * j + i, C_SEL + 72 + 128 * j + 64 * i:C_SEL + 72 + 128 * j + 64 * i + 64] = 1
    d = 255 - np.arange(512)
    n = np.maximum(d, 1).astype(np.float32)
    large = 16 + (np.log(n / np.float32(16)) / np.float32(math.log(8)) * np.float32(16)).astype(np.int32)
    bucket = np.where(d < 16, np.maximum(d, 0), np.minimum(large, 31))
    base = np.zeros((33, 512), np.float32)
    base[bucket[d >= 0], np.arange(512)[d >= 0]] = 1
    base[32, d < 0] = 1
    return c, base


def by_cols(w, cols):
    return w.reshape(8, 128, -1)[:, :, cols].transpose(1, 0, 2).reshape(128, -1)


def by_rows(w, cols, k0, k1):
    a = w.reshape(8, 128, -1)[k0:k1, :, cols].transpose(1, 0, 2).reshape(128, -1)
    return np.pad(a, ((0, 0), (0, UW - a.shape[1])))


def lay_out(i):
    units = []

    def pair(a, b):
        units.append(np.concatenate([a, b], axis=1))

    def ffn(wg, wu, wd):
        order = [("g", 0), ("g", 1)]
        for j in range(NF // 2):
            if j < NF // 2 - 1:
                order.append(("g", 2 * j + 2))
            order.append(("d", j))
            if j < NF // 2 - 1:
                order.append(("g", 2 * j + 3))
        for kind, n in order:
            if kind == "g":
                cols = slice(128 * n, 128 * n + 128)
                pair(by_cols(wg, cols), by_cols(wu, cols))
            else:
                units.append(wd.reshape(NF // 2, 2, 128, DM)[n].transpose(1, 0, 2).reshape(128, UW))

    def tiles(w, starts):
        c = [by_cols(w, slice(s, s + 128)) for s in starts]
        for n in range(0, len(c), 2):
            pair(c[n], c[n + 1])

    def square(w, order=range(4)):
        for n in order:
            units.append(w.reshape(4, 2, 128, DM)[n].transpose(1, 0, 2).reshape(128, UW))

    ffn(i["w_ffn1_gate"][0], i["w_ffn1_up"][0], i["w_ffn1_down"][0])
    w = i["w_in"][0]
    t4 = [0, 128, 256, 384]
    tiles(w, [2048, 2176])
    tiles(w, [2304, 2560])
    cols = list(range(2432, 2560)) + list(range(2688, 2840))
    for k in (0, 4):
        units.append(by_rows(w, cols, k, k + 4))
    tiles(w, [1536 + t for t in t4])
    w1 = []
    for n in ("cmp_w1_k", "cmp_w1_v"):
        c = i[n][0].reshape(2, 8, 128, 256).transpose(0, 2, 1, 3).reshape(2, 128, UW)
        w1 += [c[0], c[1]]
    for n in range(4):
        tiles(w, [(0, 256, 512, 768)[n], (128, 384, 640, 896)[n]])
        units.append(w1[n])
    for k in (0, 4):
        units.append(by_rows(w, slice(1024, 1536), k, k + 4))
    square(i["w_out"][0], (2, 3, 0, 1))
    ffn(i["w_ffn2_gate"][0], i["w_ffn2_up"][0], i["w_ffn2_down"][0])
    w = i["w_mem_kv_2"]
    tiles(w, [0, 128])
    units.append(by_rows(w, slice(256, 512), 0, 8))
    ffn(i["ffn1_w_gate_2"][0], i["ffn1_w_up_2"][0], i["ffn1_w_down_2"][0])
    tiles(i["rwkv_w_in_2"][0], [128 * t for t in range(6, 12)] + [2304, 2432] + [128 * t for t in range(6)] + [2560, 2688]
          + [128 * t for t in range(12, 18)])
    square(i["w_out_2"][0])
    ffn(i["ffn2_w_gate_2"][0], i["ffn2_w_up_2"][0], i["ffn2_w_down_2"][0])
    ffn(i["ffn1_w_gate_2"][1], i["ffn1_w_up_2"][1], i["ffn1_w_down_2"][1])
    w = i["sb_w_in_2"][0]
    tiles(w, [2304, 2432, 0, 128, 768, 896])
    for k in (0, 4):
        units.append(by_rows(w, slice(1536, 2048), k, k + 4))
    tiles(w, [256, 384, 1024, 1152, 512, 640, 1280, 1408])
    units.append(by_rows(w, slice(2048, 2304), 0, 8))
    square(i["w_out_2"][1])
    ffn(i["ffn2_w_gate_2"][1], i["ffn2_w_up_2"][1], i["ffn2_w_down_2"][1])
    assert len(units) == len(unit_kinds())
    ws = np.stack(units)

    def cols_of(v):
        return v.reshape(-1, 128).T

    def positions(v):
        return v[0].reshape(16, 128).T

    vec = np.concatenate([cols_of(i["rwkv_mu_2"][0])] + [cols_of(i[n][0]) for n in (
        "rwkv_w0_2", "rwkv_a0_2", "rwkv_k_k_2", "rwkv_k_a_2")] + [cols_of(i["rwkv_r_k_2"][0].reshape(-1))]
        + [positions(i["cmp_pos_k"]), positions(i["cmp_pos_v"])], axis=1)
    relx = np.concatenate([i["rel_bias"], np.full((1, 16), -BIG, np.float32)])
    g2 = []
    for l in range(2):
        for n in range(3):
            g2 += [i["ln_g_2"][l, n], i["ln_b_2"][l, n]]
    gains = np.stack([i["norm_ffn1"][0], i["norm_mix"][0], i["norm_ffn2"][0], i["norm_final"]] + g2)
    lora = np.concatenate([i["rwkv_w_up_2"][0], i["rwkv_a_up_2"][0]])
    k2, v2 = i["cmp_w2_k"][0].reshape(2, 128, 64), i["cmp_w2_v"][0].reshape(2, 128, 64)
    w2 = np.concatenate([k2[0], k2[0], k2[1], k2[1], v2[0], v2[1]], axis=1)
    cst, base = constants()
    return {
        "ws": ws, "cst": cst, "vec": vec, "base": base, "relx": relx, "gains": gains, "x_in": i["x"][0],
        "mem_in": i["mem_2"][0], "lora": lora, "gup": i["rwkv_g_up_2"][0],
        "lnx": np.stack([i["rwkv_lnx_g_2"][0], i["rwkv_lnx_b_2"][0]]), "w2": w2,
    }


def kernel(**inputs):
    import concourse.bacc as bacc
    from concourse.bass_utils import run_bass_kernel_spmd

    arrays = {k: np.ascontiguousarray(v) for k, v in lay_out({k: np.asarray(v) for k, v in inputs.items()}).items()}
    nc = bacc.Bacc("TRN2", target_bir_lowering=False, num_devices=1)
    aps = [nc.dram_tensor(k, a.shape, mybir.dt.from_np(a.dtype), kind="ExternalInput").ap() for k, a in arrays.items()]
    aps.append(nc.dram_tensor("out", (NT, DM), F32, kind="ExternalOutput").ap())
    build(nc, *aps)
    r = run_bass_kernel_spmd(nc, [arrays], core_ids=[0])
    return r.results[0]["out"].reshape(1, NT, DM)
```
